# Optimizing a Trainium2 kernel written in Bass

```python
import jax, jax.numpy as jnp
from jax import lax
import numpy as np

D_MODEL = 1024
BATCH = 1
SEQ = 2048
DEPTH = 1

CHUNK = 64
EPS = 1e-6
GLA_HEADS = 4
GLA_DK = 64
GLA_DV = 128
GLA_LOWRANK = 16
GLA_GATE_NORM = 16.0
GLA_QK = GLA_HEADS * GLA_DK
GLA_V = GLA_HEADS * GLA_DV
SWA_HEADS = 8
SWA_KV_HEADS = 2
SWA_HD = 64
SWA_WINDOW = 128
SWA_WIN_CHUNKS = max(1, SWA_WINDOW // CHUNK)
SWA_Q = SWA_HEADS * SWA_HD
SWA_KV = SWA_KV_HEADS * SWA_HD
MIX_WIDTH = GLA_V + SWA_Q
IN_SPLITS = (GLA_QK, GLA_QK, GLA_V, GLA_V, GLA_LOWRANK, SWA_Q, SWA_KV, SWA_KV)
IN_WIDTH = 2 * GLA_QK + 2 * GLA_V + GLA_LOWRANK + SWA_Q + 2 * SWA_KV
N_GROUPS = 4
EXP_PER_GROUP = 8
N_EXPERTS = N_GROUPS * EXP_PER_GROUP
TOP_K = 2
D_FF_EXPERT = 512
MOE_BLOCK = 256

kernel_name = "hymba_gla_swa_sink_hmoe_block"

def rms_norm(x, w):
    xf = x.astype(jnp.float32)
    y = xf * lax.rsqrt(jnp.mean(xf * xf, axis=-1, keepdims=True) + EPS)
    return (y * w.astype(jnp.float32)).astype(x.dtype)

def gla_chunked(q, k, v, log_a):
    B, S, H, dk = q.shape
    nC = S // CHUNK
    f32 = jnp.float32

    def to_chunks(t):
        return t.reshape(B, nC, CHUNK, H, t.shape[-1]).transpose(0, 3, 1, 2, 4).astype(f32)

    qc = to_chunks(q) * (dk ** -0.5)
    kc = to_chunks(k)
    vc = to_chunks(v)
    b = jnp.cumsum(to_chunks(log_a), axis=3)
    b_last = b[:, :, :, -1:]
    q_dec = qc * jnp.exp(b)
    k_inv = kc * jnp.exp(-b)
    k_end = kc * jnp.exp(b_last - b)
    causal = jnp.tril(jnp.ones((CHUNK, CHUNK), dtype=bool))
    att = jnp.einsum('bhnik,bhnjk->bhnij', q_dec, k_inv)
    att = jnp.where(causal, att, 0.0)
    o_intra = jnp.einsum('bhnij,bhnjv->bhniv', att, vc)
    d_state = jnp.einsum('bhnjk,bhnjv->bhnkv', k_end, vc)
    decay = jnp.exp(b_last[:, :, :, 0])

    def step(state, inp):
        dec, ds = inp
        return dec[..., None] * state + ds, state

    s0 = jnp.zeros((B, H, dk, vc.shape[-1]), f32)
    _, s_in = lax.scan(step, s0, (jnp.moveaxis(decay, 2, 0), jnp.moveaxis(d_state, 2, 0)))
    s_in = jnp.moveaxis(s_in, 0, 2)
    o_inter = jnp.einsum('bhnik,bhnkv->bhniv', q_dec, s_in)
    o = o_intra + o_inter
    return o.transpose(0, 2, 3, 1, 4).reshape(B, S, H, vc.shape[-1])

def swa_sink_alibi(q, k, v, sinks):
    B, S, Hq, d = q.shape
    Hkv = k.shape[2]
    R = Hq // Hkv
    nC = S // CHUNK
    W = SWA_WIN_CHUNKS
    qc = q.reshape(B, nC, CHUNK, Hkv, R, d)

    def band(t):
        tc = t.reshape(B, nC, CHUNK, Hkv, d)
        tp = jnp.pad(tc, ((0, 0), (W - 1, 0), (0, 0), (0, 0), (0, 0)))
        return jnp.concatenate([tp[:, w:w + nC] for w in range(W)], axis=2)

    kb = band(k)
    vb = band(v)
    s = jnp.einsum('bnigrd,bnjgd->bngrij', qc, kb, preferred_element_type=jnp.float32) * (d ** -0.5)
    i = jnp.arange(CHUNK)[:, None]
    j = jnp.arange(W * CHUNK)[None, :]
    dist = jnp.abs(i + (W - 1) * CHUNK - j).astype(jnp.float32)
    slopes = (2.0 ** (-8.0 * (jnp.arange(Hq, dtype=jnp.float32) + 1.0) / Hq)).reshape(Hkv, R)
    s = s - slopes[:, :, None, None] * dist
    valid = (jnp.arange(nC)[:, None] - (W - 1) + j // CHUNK) >= 0
    s = jnp.where(valid[None, :, None, None, None, :], s, -jnp.inf)
    sink = jnp.broadcast_to(sinks.astype(jnp.float32).reshape(1, 1, Hkv, R, 1, 1), s.shape[:-1] + (1,))
    p = jax.nn.softmax(jnp.concatenate([s, sink], axis=-1), axis=-1)[..., :-1]
    o = jnp.einsum('bngrij,bnjgd->bnigrd', p.astype(v.dtype), vb)
    return o.reshape(B, S, Hq * d)

def token_mixer(u, w_in, b_in, gla_w_a2, gla_b_a2, gla_norm_w, swa_sinks, w_out):
    B, S, _ = u.shape
    z = u @ w_in + b_in
    points = [int(p) for p in np.cumsum(IN_SPLITS)[:-1]]
    q_a, k_a, v_a, g_a, lr_a, q_b, k_b, v_b = jnp.split(z, points, axis=-1)
    log_a = jax.nn.log_sigmoid((lr_a @ gla_w_a2 + gla_b_a2).astype(jnp.float32)) / GLA_GATE_NORM
    o_a = gla_chunked(q_a.reshape(B, S, GLA_HEADS, GLA_DK), k_a.reshape(B, S, GLA_HEADS, GLA_DK),
                      v_a.reshape(B, S, GLA_HEADS, GLA_DV), log_a.reshape(B, S, GLA_HEADS, GLA_DK))
    o_a = o_a * lax.rsqrt(jnp.mean(o_a * o_a, axis=-1, keepdims=True) + EPS) * gla_norm_w.astype(jnp.float32)
    o_a = (o_a * jax.nn.silu(g_a.reshape(B, S, GLA_HEADS, GLA_DV).astype(jnp.float32)))
    o_a = o_a.reshape(B, S, GLA_V).astype(u.dtype)
    o_b = swa_sink_alibi(q_b.reshape(B, S, SWA_HEADS, SWA_HD), k_b.reshape(B, S, SWA_KV_HEADS, SWA_HD),
                         v_b.reshape(B, S, SWA_KV_HEADS, SWA_HD), swa_sinks).astype(u.dtype)
    return jnp.concatenate([o_a, o_b], axis=-1) @ w_out

def hier_moe(u, w_group, b_group, w_router, b_router, w_gate, w_up, w_down):
    B, S, D = u.shape
    T = B * S
    A = T * TOP_K
    hf = u.reshape(T, D)
    gp = jax.nn.softmax((hf @ w_group).astype(jnp.float32) + b_group.astype(jnp.float32), axis=-1)
    g_w, g_idx = lax.top_k(gp, 1)
    el = ((hf @ w_router).astype(jnp.float32) + b_router.astype(jnp.float32)).reshape(T, N_GROUPS, EXP_PER_GROUP)
    el = jnp.take_along_axis(el, g_idx[:, :, None], axis=1)[:, 0]
    e_val, e_idx = lax.top_k(el, TOP_K)
    gate = jax.nn.softmax(e_val, axis=-1) * g_w
    eid = (g_idx * EXP_PER_GROUP + e_idx).reshape(A)
    order = jnp.argsort(eid)
    eid_s = eid[order]
    tok_s = order // TOP_K
    gate_s = gate.reshape(A)[order]
    sizes = jnp.bincount(eid, length=N_EXPERTS)
    start = jnp.cumsum(sizes) - sizes
    psizes = (sizes + MOE_BLOCK - 1) // MOE_BLOCK * MOE_BLOCK
    pend = jnp.cumsum(psizes)
    pstart = pend - psizes
    dest = pstart[eid_s] + jnp.arange(A) - start[eid_s]
    n_blocks = -(-A // MOE_BLOCK) + N_EXPERTS
    x_pad = jnp.zeros((n_blocks * MOE_BLOCK, D), hf.dtype).at[dest].set(hf[tok_s])
    blk_e = jnp.minimum(jnp.searchsorted(pend, jnp.arange(n_blocks) * MOE_BLOCK, side='right'), N_EXPERTS - 1)

    def expert_block(args):
        xb, e = args
        return (jax.nn.silu(xb @ w_gate[e]) * (xb @ w_up[e])) @ w_down[e]

    y_pad = lax.map(expert_block, (x_pad.reshape(n_blocks, MOE_BLOCK, D), blk_e)).reshape(-1, D)
    y = y_pad[dest] * gate_s[:, None].astype(y_pad.dtype)
    out = jnp.zeros((T, D), y.dtype).at[tok_s].add(y)
    return out.reshape(B, S, D)

def setup_inputs(seed: int = 0) -> dict:
    key = jax.random.key(seed)
    ks = jax.random.split(key, 20)
    f32 = jnp.float32
    L, D = DEPTH, D_MODEL
    nrm = lambda k, shape, s: jax.random.normal(k, shape, f32) * s
    return {
        "x": jax.random.normal(ks[0], (BATCH, SEQ, D), f32),
        "norm1_w": 1.0 + nrm(ks[1], (L, D), 0.02),
        "w_in": nrm(ks[2], (L, D, IN_WIDTH), D ** -0.5),
        "b_in": nrm(ks[3], (L, IN_WIDTH), 0.01),
        "gla_w_a2": nrm(ks[4], (L, GLA_LOWRANK, GLA_QK), GLA_LOWRANK ** -0.5),
        "gla_b_a2": nrm(ks[5], (L, GLA_QK), 0.1),
        "gla_norm_w": 1.0 + nrm(ks[6], (L, GLA_DV), 0.02),
        "swa_sinks": nrm(ks[7], (L, SWA_HEADS), 0.5),
        "w_out": nrm(ks[8], (L, MIX_WIDTH, D), MIX_WIDTH ** -0.5),
        "norm2_w": 1.0 + nrm(ks[9], (L, D), 0.02),
        "w_group": nrm(ks[10], (L, D, N_GROUPS), D ** -0.5),
        "b_group": nrm(ks[11], (L, N_GROUPS), 0.01),
        "w_router": nrm(ks[12], (L, D, N_EXPERTS), D ** -0.5),
        "b_router": nrm(ks[13], (L, N_EXPERTS), 0.01),
        "w_gate": nrm(ks[14], (L, N_EXPERTS, D, D_FF_EXPERT), D ** -0.5),
        "w_up": nrm(ks[15], (L, N_EXPERTS, D, D_FF_EXPERT), D ** -0.5),
        "w_down": nrm(ks[16], (L, N_EXPERTS, D_FF_EXPERT, D), D_FF_EXPERT ** -0.5),
        "final_norm_w": 1.0 + nrm(ks[17], (D,), 0.02),
    }

def reference(x, norm1_w, w_in, b_in, gla_w_a2, gla_b_a2, gla_norm_w, swa_sinks, w_out, norm2_w,
              w_group, b_group, w_router, b_router, w_gate, w_up, w_down, final_norm_w):
    h = x
    for l in range(DEPTH):
        h = h + token_mixer(rms_norm(h, norm1_w[l]), w_in[l], b_in[l], gla_w_a2[l], gla_b_a2[l],
                            gla_norm_w[l], swa_sinks[l], w_out[l])
        h = h + hier_moe(rms_norm(h, norm2_w[l]), w_group[l], b_group[l], w_router[l], b_router[l],
                         w_gate[l], w_up[l], w_down[l])
    return rms_norm(h, final_norm_w)


_drawn_inputs = setup_inputs


def setup_inputs(seed=0):
    import zlib

    import numpy as np

    out = dict(_drawn_inputs(seed))
    spreads = {}
    factors = {'b_in': 2.802,
     'gla_norm_w': 3.571,
     'swa_sinks': 27.568,
     'b_group': 18.276,
     'b_router': 4.728,
     'final_norm_w': 8.285,
     'norm2_w': 3.578}
    for name, (base, spread) in spreads.items():
        noise = np.random.default_rng([zlib.crc32(name.encode()), seed]).standard_normal(out[name].shape)
        drawn = base * np.exp(spread * noise) if base else spread * noise
        out[name] = __import__('jax').numpy.asarray(drawn.astype(out[name].dtype))
    for name, factor in factors.items():
        out[name] = (out[name] * factor).astype(out[name].dtype)
    return out
```

```python
from contextlib import ExitStack

import concourse.bass as bass
import numpy as np
from concourse import mybir

F32 = mybir.dt.float32
BF16 = mybir.dt.bfloat16
I32 = mybir.dt.int32
ALU = mybir.AluOpType
ACT = mybir.ActivationFunctionType
AX = mybir.AxisListType

P = 128
SEQ, D = 2048, 1024
NT = SEQ // P
KD = D // P
CHUNK = 64
EPS = 1e-6
HA, DK, DV, LOWRANK = 4, 64, 128, 16
HB, HD = 8, 64
QKA, VA = HA * DK, HA * DV
NEG = -1.0e30
C_QK, C_V, C_G, C_LR, C_QB = 0, 2 * QKA, 2 * QKA + VA, 2 * QKA + 2 * VA, 2 * QKA + 2 * VA + LOWRANK
C_KB = C_QB + HB * HD
C_VB = C_KB + 2 * HD
IN_W = C_VB + 2 * HD
NG, EPG = 4, 8
NE = NG * EPG
NR = NG + NE
FF = 512
KF = FF // P
CAP = 256
NOV = 16
NSLOT = (NE + NOV) * CAP
WIDTHS = (112, 120, 128, 136, 144, 160, 192, 256)


def wait(eng, sem, n):
    if not (isinstance(n, int) and n <= 0):
        eng.wait_ge(sem, n)


def wait_apart(eng, rider, *waits):
    waits = [(sem, n if isinstance(n, int) else eng.compute_val(n)) for sem, n in waits
             if not (isinstance(n, int) and n <= 0)]
    eng.wait_ge(*rider)
    for sem, n in waits:
        eng.wait_ge(sem, n)


CREDIT = 8


class Semaphores:

    def __init__(self, nc, ctx):
        self.made, self.nc, self.ctx = {}, nc, ctx

    def __call__(self, name):
        if name not in self.made:
            self.made[name] = self.ctx.enter_context(self.nc.semaphore(name))
        return self.made[name]


JOBS = [
    ("xTa", 0, {"uT_ready": (2, 1)}), ("xTb", 0, {"uT_ready": (2, 2)}),
    ("u2Ta", 2, {"u2T_ready": (2, 1)}), ("u2Tb", 2, {"u2T_ready": (2, 2)}),
    ("qk", 0, {"qk_ready": (1, 1)}), ("qdki", 1, {"qdkiT_ready": (1, 1)}),
    ("router", 2, {"logits_ready": (1, 1)}), ("att0", 1, {"att_ready": (2, 1)}),
    ("att1", 1, {"att_ready": (2, 2)}), ("dS0", 1, {"Smid_ready": (1, 1)}),
    ("dS1", 1, {"S_ready": (1, 1)}), ("v", 0, {"v_ready": (1, 1)}),
    ("pTp", 1, {"pT_ready": (3, 1)}), ("pTc0", 1, {"pT_ready": (3, 2)}),
    ("pTc1", 1, {"pT_ready": (3, 3)}), ("g", 0, {"g_ready": (1, 1)}),
    ("og0", 1, {"og_taken": (2, 1)}), ("og1", 1, {"og_taken": (2, 2)}),
    ("ob0", 1, {"ob_taken": (2, 1)}), ("ob1", 1, {"ob_taken": (2, 2)}),
    ("kv", 0, {"kblr_taken": (1, 1), "vb_ready": (1, 1)}), ("mixAT", 1, {"mixAT_taken": (1, 1)}),
    ("la", 0, {"ls_ready": (1, 1)}), ("qb", 0, {"qbT_ready": (1, 1)}),
    ("wo0", 1, {"h_ready": (2, 1)}), ("wo1", 1, {"h_ready": (2, 2)}),
    ("sce", 0, {"s_taken": (4, 1)}), ("sco", 0, {"s_taken": (4, 2)}),
    ("spe", 0, {"s_taken": (4, 3)}), ("spo", 0, {"s_taken": (4, 4)}),
    ("bb", 0, {"decays_ready": (1, 1)}), ("bl", 0, {"dec_ready": (1, 1)}),
]
INDEX = {name: k for k, (name, _, _) in enumerate(JOBS)}


def mixer(nc, sem, bank, A, C, scratch, ctx):
    def sb(name, shape, dt=F32):
        return ctx.enter_context(nc.sbuf_tensor(name, shape, dt))

    w_in = sb("w_in_sb", [P, KD, IN_W])
    w_out = sb("w_out_sb", [P, KD, D])
    b_tm = sb("b_tm", [P, C_LR + 2 * HD])
    b_fm = sb("b_fm", [P, 6])
    norm1 = sb("norm1_sb", [P, KD])
    gnorm = sb("gnorm_sb", [P, DV])
    w_a2 = sb("w_a2_sb", [LOWRANK + 1, QKA])
    sinks = sb("sinks_sb", [P, HB])
    w_r = sb("w_r_sb", [P, KD, NR])
    b_r = sb("b_r_sb", [P, NR])
    alibi_c = sb("alibi_c", [P, HB, P])
    alibi_p = sb("alibi_p", [P, HB, CHUNK])
    cums = sb("cums", [P, 2, P])
    cind = sb("cind", [P, 2])
    causal = sb("causal", [P, P], I32)
    neghalf = sb("neghalf", [P, HA])

    x = sb("x_sb", [P, D])
    h = sb("h_sb", [P, 2, D])
    xn = sb("xn", [P, D])
    v2 = sb("v2_sb", [P, D])
    junk = sb("junk", [P, D], BF16)
    uT = sb("uT", [P, KD, P])
    u2T = sb("u2T", [P, KD, P])
    ss = sb("ss", [P, 16])
    qk = sb("qk_sb", [P, 2 * QKA])
    v = sb("v_sb", [P, 2, VA])
    g = sb("g_sb", [P, VA])
    gm = sb("gm", [P, VA])
    lrT = sb("lrT", [LOWRANK + 1, P])
    la_t = sb("la_t", [P, QKA])
    g_t = sb("g_t", [P, VA])
    ls = sb("ls_sb", [P, QKA])
    E = sb("decays", [P, 3, QKA])
    dec = sb("dec", [P, 4])
    qd = sb("qd", [P, QKA])
    ki = sb("ki", [P, QKA])
    ke = sb("ke", [P, QKA])
    qdkiT = sb("qdkiT", [P, 4, P])
    attm = sb("attm", [P, HA, P])
    S = sb("S", [P, 2, 2, DV])
    Smid = sb("Smid", [P, 2, DV])
    mixA = sb("mixA", [P, VA])
    mixT = sb("mixT", [P, KD, P])
    qbT = sb("qbT", [P, 4, P])
    kb = sb("kb_sb", [P, 2, 2, P])
    vb = sb("vb_sb", [P, 2, 2 * HD])
    vlo = sb("vlo", [CHUNK, 2 * HD])
    sc = sb("sc", [P, HB, P])
    sp_ = sb("sp_", [P, HB, CHUNK])
    sm = sb("sm", [P, 10, HB])
    pTp = sb("pTp", [P, 4, P])
    pTc = sb("pTc", [P, HB, P])
    nought = sb("nought", [P, 256])
    ident, norm2, logits = C["ident"], C["norm2"], C["logits"]
    m_c, m_p, m_, nm, den_c, den_p, esink, den, rden = (sm[:, n, :] for n in range(9))

    b_tm_vb = b_tm[:, C_LR:C_LR + 2 * HD]

    def loads(sp):
        sp.dma_start(x[:, :], A["x"][0:P, :]).then_inc(sem("x_loaded"), 16)
        first = [(ident, A["c_ident"]), (norm1[:, :], A["norm1_t"]), (norm2, A["norm2_t"]),
                 (neghalf[:, :], A["c_neghalf"])]
        for dst, src in first:
            sp.dma_start(dst, src).then_inc(sem("first_consts"), 16)
        for lo, hi in ((0, C_V), (C_V, C_G), (C_G, C_LR), (C_LR, IN_W)):
            sp.dma_start(w_in[:, :, lo:hi],
                         A["w_in"][0, :, lo:hi].rearrange("(k p) n -> p k n", p=P)).then_inc(sem(f"w_in_loaded{lo}"), 16)
            if lo == 0:
                for dst, src in [(b_tm[:, 0:C_LR], A["b_in"][0:1, 0:C_LR].to_broadcast([P, C_LR])),
                                 (b_tm_vb, A["b_in"][0:1, C_VB:IN_W].to_broadcast([P, 2 * HD])),
                                 (b_fm[:, :], A["b_fm"]), (w_a2[:, :], A["w_a2"]),
                                 (sinks[:, :], A["swa_sinks"].to_broadcast([P, HB])),
                                 (gnorm[:, :], A["gla_norm_w"].to_broadcast([P, DV])),
                                 (cums[:, :, :], A["c_cums"]), (cind[:, :], A["c_cind"]),
                                 (causal[:, :], A["c_causal"]),
                                 (alibi_c[:, :, :], A["c_alibi"][:, :, 0:P]),
                                 (alibi_p[:, :, :], A["c_alibi"][:, :, P:P + CHUNK])]:
                    sp.dma_start(dst, src).then_inc(sem("consts"), 16)
        sp.dma_start(w_out[:, :, :], A["w_out"][0].rearrange("(k p) n -> p k n", p=P)).then_inc(sem("w_out_loaded"), 16)
        sp.dma_start(w_r[:, :, 0:NG], A["w_group"][0].rearrange("(k p) n -> p k n", p=P)).then_inc(sem("w_out_loaded"), 16)
        sp.dma_start(w_r[:, :, NG:NR], A["w_router"][0].rearrange("(k p) n -> p k n", p=P)).then_inc(sem("w_out_loaded"), 16)
        sp.dma_start(b_r[:, 0:NG], A["b_group"].to_broadcast([P, NG])).then_inc(sem("w_out_loaded"), 16)
        sp.dma_start(b_r[:, NG:NR], A["b_router"].to_broadcast([P, NE])).then_inc(sem("w_out_loaded"), 16)

    def clear_y(sp, i):
        blocks = scratch["y"].rearrange("(b p) (r c) -> b p r c", p=P, c=256)
        src = nought[:, None, :].to_broadcast([P, D // 256, 256])
        n = NE // NT
        for m in range(n):
            for b in (2 * (n * i + m) + 1, 2 * NE + n * i + m):
                dst = blocks[b] if isinstance(b, int) else blocks[bass.ds(b, 1)].rearrange("o p r c -> (o p) r c")
                sp.dma_start(dst, src).then_inc(sem("y_cleared"), 16)

    FIRST, CONSTS, W_OUT = 4 * 16, 11 * 16, 5 * 16

    rider = (sem("first_consts"), FIRST)

    def tile_rows(ap, t):
        return ap[t * P:(t + 1) * P, :] if isinstance(t, int) else ap[bass.ds(t * P, P), :]

    def sp_iter(sp, i, par):
        if not isinstance(i, int) or i + 1 < NT:
            wait_apart(sp, rider, (sem("xn_ready"), i + 1))
            nxt = i + 1 if isinstance(i, int) else (i + 1) & (NT - 1)
            sp.dma_start(x[:, :], tile_rows(A["x"], nxt)).then_inc(sem("x_loaded"), 16)
        if not isinstance(i, int) or i < NT:
            clear_y(sp, i)
            wait_apart(sp, rider, (sem("h_stored"), 16 * (i - 1)),
                       (sem("v2_ready"), i - 1))
            sp.dma_start(h[:, par, :], tile_rows(A["x"], i)).then_inc(sem("xr_loaded"), 16)
        if not isinstance(i, int) or 1 <= i <= NT:
            wait_apart(sp, rider, (sem("h_ready"), 2 * i))
            sp.dma_start(tile_rows(scratch["h"], i - 1), h[:, 1 - par, :]).then_inc(sem("h_stored"), 16)
            wait_apart(sp, rider, (sem("v2_ready"), i))
            sp.dma_start(tile_rows(scratch["v2"], i - 1), v2[:, :]).then_inc(sem("v2_stored"), 16)

    def runs(k, i):
        return not isinstance(i, int) or 0 <= i - JOBS[k][1] < NT

    def bank_free(k, i):
        j, it = k, i
        for _ in range(12):
            j -= 8
            if j < 0:
                j, it = j + len(JOBS), it - 1
            if isinstance(it, int) and it < 0:
                return []
            if runs(j, it):
                name, lag, taken = JOBS[j]
                if name in ("spe", "spo") and isinstance(it, int) and it == 0:
                    continue
                return [(sem(s), (it - lag) * per + nth) for s, (per, nth) in taken.items()]
        return []

    def pe_iter(pe, i, par):
        bk = {name: bank[k % 8] for k, (name, _, _) in enumerate(JOBS)}

        def on(name):
            k = INDEX[name]
            if not runs(k, i):
                return False
            for s, n in bank_free(k, i):
                wait(pe, s, n)
            return True

        def transposes(name, src, n):
            for c in range(n):
                m = pe.transpose(bk[name][:, c * P:(c + 1) * P], src(c), ident)
            m.then_inc(sem(name + "_done"), 1)

        def project(name, lo, hi, col=0, stop_inc=True):
            for k in range(KD):
                m = pe.matmul(bk[name][:, col:col + hi - lo], uT[:, k, :], w_in[:, k, lo:hi],
                              start=k == 0, stop=k == KD - 1)
            return m

        def project_T(name, lo, hi, col):
            for k in range(KD):
                m = pe.matmul(bk[name][0:hi - lo, col:col + P], w_in[:, k, lo:hi], uT[:, k, :],
                              start=k == 0, stop=k == KD - 1)
            return m

        if on("xTa"):
            wait(pe, sem("xn_ready"), i + 1)
            transposes("xTa", lambda c: xn[:, c * P:(c + 1) * P], 4)
        if on("xTb"):
            transposes("xTb", lambda c: xn[:, (4 + c) * P:(5 + c) * P], 4)
        if on("u2Ta"):
            wait(pe, sem("v2_ready"), i - 1)
            transposes("u2Ta", lambda c: v2[:, c * P:(c + 1) * P], 4)
        if on("u2Tb"):
            transposes("u2Tb", lambda c: v2[:, (4 + c) * P:(5 + c) * P], 4)
        if on("qk"):
            if isinstance(i, int) and i == 0:
                wait(pe, sem(f"w_in_loaded{C_QK}"), 16)
            wait(pe, sem("uT_ready"), 2 * i + 2)
            project("qk", C_QK, C_V).then_inc(sem("qk_done"), 1)
        if on("qdki"):
            wait(pe, sem("qdki_ready"), i)
            for c in range(2):
                pe.transpose(bk["qdki"][:, c * P:(c + 1) * P], qd[:, c * P:(c + 1) * P], ident)
            for c in range(2):
                m = pe.transpose(bk["qdki"][:, (2 + c) * P:(3 + c) * P], ki[:, c * P:(c + 1) * P], ident)
            m.then_inc(sem("qdki_done"), 1)
        if on("router"):
            if isinstance(i, int):
                wait(pe, sem("w_out_loaded"), W_OUT)
            wait(pe, sem("u2T_ready"), 2 * (i - 2) + 2)
            for k in range(KD):
                m = pe.matmul(bk["router"][:, 0:NR], u2T[:, k, :], w_r[:, k, :], start=k == 0, stop=k == KD - 1)
            m.then_inc(sem("router_done"), 1)
        for a in range(2):
            name = f"att{a}"
            if on(name):
                wait(pe, sem("qdkiT_ready"), i)
                r = slice(64 * a, 64 * a + 64)
                for pr in range(2):
                    m = pe.matmul(bk[name][:, pr * P:(pr + 1) * P], qdkiT[r, 2 + pr, :], qdkiT[r, pr, :],
                                  start=True, stop=True)
                m.then_inc(sem("att_done"), 1)
        for c in range(2):
            name = f"dS{c}"
            if runs(INDEX[name], i):
                wait_apart(pe, rider, *bank_free(INDEX[name], i), (sem("ke_ready"), i))
                r = slice(64 * c, 64 * c + 64)
                for hh in range(HA):
                    a, pr = hh % 2, hh // 2
                    m = pe.matmul(bk[name][64 * a:64 * a + 64, pr * DV:(pr + 1) * DV],
                                  ke[r, hh * DK:(hh + 1) * DK], v[r, 1 - par, hh * DV:(hh + 1) * DV],
                                  start=True, stop=True)
                m.then_inc(sem("dS_done"), 1)
        if on("v"):
            if isinstance(i, int) and i == 0:
                wait(pe, sem(f"w_in_loaded{C_V}"), 16)
            project("v", C_V, C_G).then_inc(sem("v_done"), 1)
        if on("pTp"):
            wait(pe, sem("p_ready"), 2 * i)
            transposes("pTp", lambda c: sp_[:, 2 * c:2 * c + 2, :].rearrange("p h j -> p (h j)"), 4)
        for n in range(2):
            if on(f"pTc{n}"):
                transposes(f"pTc{n}", lambda c: sc[:, 4 * n + c, :], 4)
        if on("g"):
            if isinstance(i, int) and i == 0:
                wait(pe, sem(f"w_in_loaded{C_G}"), 16)
            project("g", C_G, C_LR).then_inc(sem("g_done"), 1)
        for a in range(2):
            name = f"og{a}"
            if on(name):
                wait(pe, sem("att_ready"), 2 * (i - 1) + a + 1)
                wait(pe, sem("Smid_ready"), i)
                for pr in range(2):
                    hh = 2 * pr + a
                    o = slice(pr * DV, (pr + 1) * DV)
                    r = slice(64 * a, 64 * a + 64)
                    pe.matmul(bk[name][:, o], attm[:, hh, :], v[:, 1 - par, hh * DV:(hh + 1) * DV],
                              start=True, stop=False, skip_group_check=True)
                    pe.matmul(bk[name][0:64, o], qdkiT[r, pr, 0:64], S[r, 1 - par, pr, :],
                              start=False, stop=True, skip_group_check=True)
                    m = pe.matmul(bk[name][64:128, o], qdkiT[r, pr, 64:128], Smid[r, pr, :],
                                  start=False, stop=True, skip_group_check=True)
                m.then_inc(sem("og_done"), 1)
        for a in range(2):
            name = f"ob{a}"
            if on(name):
                wait(pe, sem("pT_ready"), 3 * i)
                wait(pe, sem("vlo_ready"), i - 1)
                r = slice(64 * a, 64 * a + 64)
                first_tile = isinstance(i, int) and i == 1
                for pr in range(4):
                    hh = 2 * pr + a
                    gg = hh // 4
                    m = pe.matmul(bk[name][r, pr * P:(pr + 1) * P], vb[:, 1 - par, gg * HD:(gg + 1) * HD],
                                  pTc[:, hh, :], start=True, stop=first_tile, skip_group_check=True)
                    if not first_tile:
                        vp = vlo[:, gg * HD:(gg + 1) * HD] if a == 0 else vb[64:128, par, gg * HD:(gg + 1) * HD]
                        m = pe.matmul(bk[name][r, pr * P:(pr + 1) * P], vp, pTp[r, pr, :],
                                      start=False, stop=True, skip_group_check=True)
                m.then_inc(sem("ob_done"), 1)
        if on("kv"):
            if isinstance(i, int) and i == 0:
                wait(pe, sem(f"w_in_loaded{C_LR}"), 16)
            project_T("kv", C_KB, C_VB, 0)
            project_T("kv", C_LR, C_QB, P)
            project("kv", C_VB, IN_W, col=2 * P).then_inc(sem("kv_done"), 1)
        if on("mixAT"):
            wait(pe, sem("mixA_ready"), i)
            transposes("mixAT", lambda c: mixA[:, c * P:(c + 1) * P], 4)
        if on("la"):
            wait(pe, sem("lrT_ready"), i + 1)
            pe.matmul(bk["la"][:, 0:QKA], lrT[:, :], w_a2[:, :], start=True, stop=True).then_inc(sem("la_done"), 1)
        if on("qb"):
            for m_ in range(4):
                m = project_T("qb", C_QB + m_ * P, C_QB + (m_ + 1) * P, m_ * P)
            m.then_inc(sem("qb_done"), 1)
        for n in range(2):
            if on(f"wo{n}"):
                if isinstance(i, int) and i == 1 and n == 0:
                    wait(pe, sem("w_out_loaded"), W_OUT)
                wait(pe, sem("ob_taken"), 2 * i)
                wait(pe, sem("mixAT_taken"), i)
                for k in range(KD):
                    m = pe.matmul(bk[f"wo{n}"][:, :], mixT[:, k, :], w_out[:, k, n * 512:(n + 1) * 512],
                                  start=k == 0, stop=k == KD - 1)
                m.then_inc(sem("wo_done"), 1)
        for name, a, prev in (("sce", 0, False), ("sco", 1, False), ("spe", 0, True), ("spo", 1, True)):
            if prev and isinstance(i, int) and i == 0:
                continue
            if on(name):
                wait(pe, sem("qbT_ready"), i + 1)
                wait(pe, sem("kb_ready"), i + 1)
                r = slice(64 * a, 64 * a + 64)
                w = CHUNK if prev else P
                for pr in range(4):
                    gg = (2 * pr + a) // 4
                    keys = kb[r, 1 - par, gg, CHUNK:P] if prev else kb[r, par, gg, :]
                    m = pe.matmul(bk[name][:, pr * w:(pr + 1) * w], qbT[r, pr, :], keys, start=True, stop=True)
                m.then_inc(sem("s_done"), 1)
        if on("bb"):
            wait(pe, sem("ls_ready"), i + 1)
            for n in range(2):
                m = pe.matmul(bk["bb"][:, n * QKA:(n + 1) * QKA], cums[:, n, :], ls[:, :], start=True, stop=True)
            m.then_inc(sem("bb_done"), 1)
        if on("bl"):
            for pr in range(2):
                m = pe.matmul(bk["bl"][:, 2 * pr:2 * pr + 2], ls[:, pr * P:(pr + 1) * P], cind[:, :],
                              start=True, stop=True)
            m.then_inc(sem("bl_done"), 1)

    BK = {name: bank[k % 8] for k, (name, _, _) in enumerate(JOBS)}

    def s_count(i, n):
        return n if isinstance(i, int) and i == 0 else 4 * i - 2 + n

    def act_iter(act, i, par):
        old = not isinstance(i, int) or 1 <= i <= NT
        new = not isinstance(i, int) or i < NT

        def square(t):
            wait(act, sem("x_loaded"), 16 * (t + 1))
            wait(act, sem("ss2_ready"), t - 2)
            act.activation(junk[:, :], x[:, :], ACT.Square, accum_out=ss[:, 0:1]).then_inc(sem("ss1_ready"), 1)

        if isinstance(i, int) and i == 0:
            square(0)
        if old:
            wait(act, sem("qdki_done"), i)
            wait(act, sem("og_done"), 2 * (i - 1))
            act.activation(qdkiT[:, :, :].rearrange("p a b -> p (a b)"), BK["qdki"][:, :], ACT.Copy)\
                .then_inc(sem("qdkiT_ready"), 1)
            for n, (name, dst) in enumerate((("pTp", pTp[:, :, :]), ("pTc0", pTc[:, 0:4, :]), ("pTc1", pTc[:, 4:8, :]))):
                wait(act, sem(name + "_done"), i)
                wait(act, sem("ob_done"), 2 * (i - 1))
                act.activation(dst.rearrange("p a b -> p (a b)"), BK[name][:, :], ACT.Copy).then_inc(sem("pT_ready"), 1)
        if not isinstance(i, int) or i + 1 < NT:
            wait(act, sem("rstd1_ready"), i + 1)
            square(i + 1)
        if old:
            for a in range(2):
                wait(act, sem("og_done"), 2 * (i - 1) + a + 1)
                if a == 0:
                    wait(act, sem("ss1_ready"), min(i + 2, NT) if isinstance(i, int) else i + 2)
                for pr in range(2):
                    hh = 2 * pr + a
                    m = act.activation(junk[:, hh * DV:(hh + 1) * DV], BK[f"og{a}"][:, pr * DV:(pr + 1) * DV], ACT.Square,
                                       accum_out=ss[:, 4 + hh:5 + hh])
                m.then_inc(sem("ssg_ready"), 1)
            for a in range(2):
                wait(act, sem("ob_done"), 2 * (i - 1) + a + 1)
                wait(act, sem("wo_done"), 2 * (i - 1))
                r = slice(64 * a, 64 * a + 64)
                act.activation(mixT[r, 4:8, :].rearrange("p a b -> p (a b)"), BK[f"ob{a}"][r, :], ACT.Copy)\
                    .then_inc(sem("ob_taken"), 1)
        if new:
            wait(act, sem("kv_done"), i + 1)
            if isinstance(i, int) and i == 0:
                wait(act, sem("consts"), CONSTS)
                wait(act, sem("filled"), 2)
            wait(act, sem("s_done"), s_count(i, 0))
            wait(act, sem("la_done"), i)
            act.activation(lrT[0:LOWRANK, :], BK["kv"][0:LOWRANK, P:2 * P], ACT.Identity, bias=b_fm[0:LOWRANK, 5:6])\
                .then_inc(sem("lrT_ready"), 1)
            act.activation(kb[0:64, par, 0, :], BK["kv"][0:64, 0:P], ACT.Identity, bias=b_fm[0:64, 4:5])\
                .then_inc(sem("kb_halves"), 1)
            act.activation(kb[64:128, par, 1, :], BK["kv"][64:128, 0:P], ACT.Identity, bias=b_fm[64:128, 4:5])\
                .then_inc(sem("kblr_taken"), 1)
        if old:
            wait(act, sem("mixAT_done"), i)
            act.activation(mixT[:, 0:4, :].rearrange("p a b -> p (a b)"), BK["mixAT"][:, :], ACT.Copy)\
                .then_inc(sem("mixAT_taken"), 1)
        if new:
            wait(act, sem("la_done"), i + 1)
            wait(act, sem("ls_ready"), i)
            act.activation(la_t[:, :], BK["la"][:, 0:QKA], ACT.Abs).then_inc(sem("la_abs"), 1)
            act.wait_ge(sem("la_abs"), 2 * i + 1)
            act.activation(la_t[:, :], la_t[:, :], ACT.Exp, scale=-1.0).then_inc(sem("la_abs"), 1)
            act.wait_ge(sem("la_abs"), 2 * i + 2)
            act.activation(la_t[:, :], la_t[:, :], ACT.Ln, bias=1.0).then_inc(sem("la_ln"), 1)
            wait(act, sem("qb_done"), i + 1)
            for n in range(4):
                m = act.activation(qbT[:, n, :], BK["qb"][:, n * P:(n + 1) * P], ACT.Identity, bias=b_fm[:, n:n + 1])
            m.then_inc(sem("qbT_ready"), 1)
            wait(act, sem("g_ready"), i + 1)
            wait(act, sem("gm_ready"), i)
            act.activation(g_t[:, :], g[:, :], ACT.Abs).then_inc(sem("g_abs"), 1)
            act.wait_ge(sem("g_abs"), 2 * i + 1)
            act.activation(g_t[:, :], g_t[:, :], ACT.Exp, scale=-1.0).then_inc(sem("g_abs"), 1)
            act.wait_ge(sem("g_abs"), 2 * i + 2)
            act.activation(g_t[:, :], g_t[:, :], ACT.Ln, bias=1.0).then_inc(sem("g_ln"), 1)
        if old:
            wait(act, sem("h_ready"), 2 * i)
            wait(act, sem("ssg_ready"), 2 * i)
            act.activation(junk[:, :], h[:, 1 - par, :], ACT.Square, accum_out=ss[:, 8:9]).then_inc(sem("ss2_ready"), 1)
        if new:
            wait(act, sem("lsg_ready"), i + 1)
            act.activation(g_t[:, :], g_t[:, :], ACT.Exp).then_inc(sem("sig_ready"), 1)
            wait(act, sem("bb_done"), i + 1)
            wait(act, sem("ke_ready"), i)
            act.activation(E[:, 0:2, :].rearrange("p a b -> p (a b)"), BK["bb"][:, :], ACT.Exp)
            act.activation(E[:, 2, :], BK["bb"][:, 0:QKA], ACT.Exp, scale=-1.0).then_inc(sem("decays_ready"), 1)
            wait(act, sem("bl_done"), i + 1)
            wait(act, sem("S_ready"), i)
            act.activation(dec[:, :], BK["bl"][:, 0:4], ACT.Exp).then_inc(sem("dec_ready"), 1)
            wait(act, sem("nm_ready"), i + 1)
            for hh in range(HB):
                act.activation(sc[:, hh, :], sc[:, hh, :], ACT.Exp, bias=nm[:, hh:hh + 1], accum_out=den_c[:, hh:hh + 1])
                act.activation(sp_[:, hh, :], sp_[:, hh, :], ACT.Exp, bias=nm[:, hh:hh + 1], accum_out=den_p[:, hh:hh + 1])
            act.activation(esink, esink, ACT.Exp).then_inc(sem("exps_ready"), 1)

    def dve_iter(v_, i, par):
        old = not isinstance(i, int) or 1 <= i <= NT
        new = not isinstance(i, int) or i < NT
        old2 = not isinstance(i, int) or 2 <= i
        dve = nc.vector

        def normalise_x(t):
            wait(v_, sem("rstd1_ready"), t + 1)
            if not isinstance(t, int) or t >= 1:
                wait(v_, sem("xTb_done"), t)
            dve.tensor_scalar(xn[:, :], x[:, :], ss[:, 1:2], None, ALU.mult).then_inc(sem("xn_ready"), 1)

        if isinstance(i, int) and i == 0:
            dve.memset(nought[:, :], 0.0).then_inc(sem("filled"), 1)
            dve.memset(lrT[:, :], 1.0).then_inc(sem("filled"), 1)
            dve.memset(attm[:, :, :], 0.0).then_inc(sem("filled"), 1)
            dve.memset(S[:, 0, :, :], 0.0).then_inc(sem("filled"), 1)
            wait(v_, sem("first_consts"), FIRST)
            normalise_x(0)
        if new:
            for n, name in enumerate(("xTa", "xTb")):
                wait(v_, sem(name + "_done"), i + 1)
                wait(v_, sem("qb_done"), i)
                dve.tensor_tensor(uT[:, 4 * n:4 * n + 4, :], BK[name][:, :].rearrange("p (a b) -> p a b", a=4),
                                  norm1[:, 4 * n:4 * n + 4].unsqueeze(2).to_broadcast([P, 4, P]), ALU.mult)\
                    .then_inc(sem("uT_ready"), 1)
        if old2:
            for n, name in enumerate(("u2Ta", "u2Tb")):
                wait(v_, sem(name + "_done"), i - 1)
                wait(v_, sem("router_done"), i - 2)
                dve.tensor_tensor(u2T[:, 4 * n:4 * n + 4, :], BK[name][:, :].rearrange("p (a b) -> p a b", a=4),
                                  norm2[:, 4 * n:4 * n + 4].unsqueeze(2).to_broadcast([P, 4, P]), ALU.mult)\
                    .then_inc(sem("u2T_ready"), 1)
        if old:
            wait(v_, sem("decays_ready"), i)
            wait(v_, sem("qdki_done"), i - 1)
            wait(v_, sem("dS_done"), 2 * (i - 1))
            dve.scalar_tensor_tensor(qd[:, :], qk[:, 0:QKA], DK ** -0.5, E[:, 0, :], ALU.mult, ALU.mult)
            dve.tensor_tensor(ki[:, :], qk[:, QKA:], E[:, 2, :], ALU.mult).then_inc(sem("qdki_ready"), 1)
            dve.tensor_tensor(ke[:, :], qk[:, QKA:], E[:, 1, :], ALU.mult).then_inc(sem("ke_ready"), 1)
            wait(v_, sem("exps_ready"), i)
            dve.tensor_tensor(den, den_c, den_p, ALU.add).then_inc(sem("den_steps"), 1)
            v_.wait_ge(sem("den_steps"), 3 * (i - 1) + 1)
            dve.tensor_tensor(den, den, esink, ALU.add).then_inc(sem("den_steps"), 1)
            v_.wait_ge(sem("den_steps"), 3 * (i - 1) + 2)
            dve.reciprocal(rden, den).then_inc(sem("den_steps"), 1)
            v_.wait_ge(sem("den_steps"), 3 * (i - 1) + 3)
            dve.tensor_tensor(sp_[:, :, :], sp_[:, :, :], rden.unsqueeze(2).to_broadcast([P, HB, CHUNK]), ALU.mult)\
                .then_inc(sem("p_ready"), 1)
            dve.tensor_tensor(sc[:, :, :], sc[:, :, :], rden.unsqueeze(2).to_broadcast([P, HB, P]), ALU.mult)\
                .then_inc(sem("p_ready"), 1)
        if new:
            if isinstance(i, int) and i == 0:
                wait(v_, sem("consts"), CONSTS)
            wait(v_, sem("qk_done"), i + 1)
            dve.tensor_tensor(qk[:, :], BK["qk"][:, :], b_tm[:, C_QK:C_V], ALU.add).then_inc(sem("qk_ready"), 1)
        if old2:
            wait(v_, sem("router_done"), i - 1)
            t = i - 2
            dst = logits[:, t, :] if isinstance(t, int) else logits[:, bass.ds(t, 1), :].rearrange("p o n -> p (o n)")
            dve.tensor_tensor(dst, BK["router"][:, 0:NR], b_r[:, :], ALU.add).then_inc(sem("logits_ready"), 1)
        if old:
            for a in range(2):
                if isinstance(i, int) and i == 1:
                    wait(v_, sem("filled"), 4)
                wait_apart(v_, rider, (sem("og_done"), 2 * (i - 1)),
                           (sem("att_done"), 2 * (i - 1) + a + 1))
                dve.copy_predicated(attm[:, a::2, :], causal[:, None, :].to_broadcast([P, 2, P]),
                                    BK[f"att{a}"][:, 0:2 * P].rearrange("p (a b) -> p a b", a=2))\
                    .then_inc(sem("att_ready"), 1)
            wait(v_, sem("dS_done"), 2 * (i - 1) + 2)
            wait(v_, sem("dec_ready"), i)
            for pr in range(2):
                m = dve.scalar_tensor_tensor(Smid[:, pr, :], S[:, 1 - par, pr, :], dec[:, 2 * pr:2 * pr + 1],
                                             BK["dS0"][:, pr * DV:(pr + 1) * DV], ALU.mult, ALU.add)
            m.then_inc(sem("Smid_ready"), 1)
            v_.wait_ge(sem("Smid_ready"), i)
            for pr in range(2):
                m = dve.scalar_tensor_tensor(S[:, par, pr, :], Smid[:, pr, :], dec[:, 2 * pr + 1:2 * pr + 2],
                                             BK["dS1"][:, pr * DV:(pr + 1) * DV], ALU.mult, ALU.add)
            m.then_inc(sem("S_ready"), 1)
        if new:
            wait(v_, sem("v_done"), i + 1)
            dve.tensor_tensor(v[:, par, :], BK["v"][:, :], b_tm[:, C_V:C_G], ALU.add).then_inc(sem("v_ready"), 1)
            if not isinstance(i, int) or i + 1 < NT:
                normalise_x(i + 1)
            wait(v_, sem("g_done"), i + 1)
            wait(v_, sem("gm_ready"), i)
            dve.tensor_tensor(g[:, :], BK["g"][:, :], b_tm[:, C_G:C_LR], ALU.add).then_inc(sem("g_ready"), 1)
        if old:
            wait(v_, sem("rstdg_ready"), i)
            wait(v_, sem("mixAT_done"), i - 1)
            wait(v_, sem("gm_ready"), i)
            for a in range(2):
                dve.tensor_tensor(mixA[:, :].rearrange("p (a c b) -> p a c b", a=2, c=2)[:, :, a, :],
                                  BK[f"og{a}"][:, 0:2 * DV].rearrange("p (a b) -> p a b", a=2),
                                  ss[:, 12 + a:16:2].unsqueeze(2).to_broadcast([P, 2, DV]), ALU.mult)\
                    .then_inc(sem("og_taken"), 1)
            v_.wait_ge(sem("og_taken"), 2 * i)
            dve.tensor_tensor(mixA[:, :], mixA[:, :], gm[:, :], ALU.mult).then_inc(sem("mixA_ready"), 1)
        if new:
            wait(v_, sem("kblr_taken"), i + 1)
            wait(v_, sem("ob_done"), 2 * i)
            dve.tensor_tensor(vb[:, par, :], BK["kv"][:, 2 * P:3 * P], b_tm_vb, ALU.add).then_inc(sem("vb_ready"), 1)
            if not isinstance(i, int) or i >= 1:
                dve.tensor_copy(vlo[:, :], vb[64:128, 1 - par, :]).then_inc(sem("vlo_ready"), 1)
            wait(v_, sem("kb_halves"), i + 1)
            dve.tensor_copy(kb[64:128, par, 0, :], kb[0:64, par, 0, :])
            dve.tensor_copy(kb[0:64, par, 1, :], kb[64:128, par, 1, :]).then_inc(sem("kb_ready"), 1)
            wait(v_, sem("la_ln"), i + 1)
            wait(v_, sem("bl_done"), i)
            dve.scalar_tensor_tensor(ls[:, :], BK["la"][:, 0:QKA], 0.0, la_t[:, :], ALU.min, ALU.subtract)\
                .then_inc(sem("ls_ready"), 1)
        if old:
            wait(v_, sem("xr_loaded"), 16 * i)
            for n in range(2):
                wait(v_, sem("wo_done"), 2 * (i - 1) + n + 1)
                hs = h[:, 1 - par, n * 512:(n + 1) * 512]
                dve.tensor_tensor(hs, BK[f"wo{n}"][:, :], hs, ALU.add).then_inc(sem("h_ready"), 1)
        if new:
            wait(v_, sem("g_ln"), i + 1)
            dve.scalar_tensor_tensor(g_t[:, :], g[:, :], 0.0, g_t[:, :], ALU.min, ALU.subtract).then_inc(sem("lsg_ready"), 1)
            wait(v_, sem("pTc1_done"), i)
            for n, (name, w, dst, ali) in enumerate((("sce", P, sc, alibi_c), ("sco", P, sc, alibi_c),
                                                     ("spe", CHUNK, sp_, alibi_p), ("spo", CHUNK, sp_, alibi_p))):
                if n >= 2 and isinstance(i, int) and i == 0:
                    dve.memset(sp_[:, n % 2::2, :], NEG).then_inc(sem("s_taken"), 1)
                    continue
                wait(v_, sem("s_done"), s_count(i, n + 1))
                dve.scalar_tensor_tensor(dst[:, n % 2::2, :], BK[name][:, 0:4 * w].rearrange("p (a b) -> p a b", a=4),
                                         HD ** -0.5, ali[:, n % 2::2, :], ALU.mult, ALU.add).then_inc(sem("s_taken"), 1)
            v_.wait_ge(sem("s_taken"), 4 * i + 4)
            dve.tensor_reduce(m_c, sc[:, :, :], AX.X, ALU.max).then_inc(sem("max_steps"), 1)
            dve.tensor_reduce(m_p, sp_[:, :, :], AX.X, ALU.max).then_inc(sem("max_steps"), 1)
            v_.wait_ge(sem("max_steps"), 4 * i + 2)
            dve.tensor_tensor(m_, m_c, m_p, ALU.max).then_inc(sem("max_steps"), 1)
            v_.wait_ge(sem("max_steps"), 4 * i + 3)
            dve.tensor_tensor(m_, m_, sinks[:, :], ALU.max).then_inc(sem("max_steps"), 1)
            v_.wait_ge(sem("max_steps"), 4 * i + 4)
            dve.tensor_tensor(esink, sinks[:, :], m_, ALU.subtract)
            dve.tensor_scalar(nm, m_, -1.0, None, ALU.mult).then_inc(sem("nm_ready"), 1)
        if old:
            wait(v_, sem("rstd2_ready"), i)
            wait(v_, sem("v2_stored"), 16 * (i - 1))
            wait(v_, sem("u2Tb_done"), i - 1)
            dve.tensor_scalar(v2[:, :], h[:, 1 - par, :], ss[:, 9:10], None, ALU.mult).then_inc(sem("v2_ready"), 1)

    def pool_iter(po, i, par):
        old = not isinstance(i, int) or 1 <= i <= NT
        new = not isinstance(i, int) or i < NT
        pool = nc.gpsimd

        def rstd(ready, done, step, n_ready, n_done, src, dst, width, count, *also):
            wait_apart(po, rider, (sem(ready), n_ready), *also)
            pool.tensor_scalar(src, src, 1.0 / count, EPS, ALU.mult, ALU.add).then_inc(sem(step), 1)
            wait(po, sem(step), n_done)
            pool.tensor_tensor(dst, src, neghalf[:, 0:width], ALU.pow).then_inc(sem(done), 1)

        def rstd_x(t):
            rstd("ss1_ready", "rstd1_ready", "mean1", t + 1, t + 1, ss[:, 0:1], ss[:, 1:2], 1, D,
                 (sem("xn_ready"), t))

        if isinstance(i, int) and i == 0:
            rstd_x(0)
        if not isinstance(i, int) or i + 1 < NT:
            rstd_x(i + 1)
        if old:
            rstd("ssg_ready", "rstdg_ready", "meang", 2 * i, i, ss[:, 4:8], ss[:, 12:16], HA, DV,
                 (sem("mixA_ready"), i - 1))
            rstd("ss2_ready", "rstd2_ready", "mean2", i, i, ss[:, 8:9], ss[:, 9:10], 1, D,
                 (sem("v2_ready"), i - 1))
        if new:
            if isinstance(i, int) and i == 0:
                wait(po, sem("consts"), CONSTS)
            wait(po, sem("mixA_ready"), i)
            wait(po, sem("sig_ready"), i + 1)
            pool.tensor_tensor(gm[:, :], g[:, :], g_t[:, :], ALU.mult).then_inc(sem("gm_step"), 1)
            po.wait_ge(sem("gm_step"), i + 1)
            pool.tensor_tensor(gm[:, :].rearrange("p (a b) -> p a b", a=HA), gm[:, :].rearrange("p (a b) -> p a b", a=HA),
                               gnorm[:, None, :].to_broadcast([P, HA, DV]), ALU.mult).then_inc(sem("gm_ready"), 1)

    return loads, sp_iter, pe_iter, act_iter, dve_iter, pool_iter


def pipeline(eng, step):
    step(eng, 0, 0)
    step(eng, 1, 1)
    with eng.Fori(1, NT // 2) as pair:
        step(eng, 2 * pair, 0)
        step(eng, 2 * pair + 1, 1)
    step(eng, NT, 0)
    step(eng, NT + 1, 1)


def host_constants():
    i, j = np.arange(P)[None, :], np.arange(P)[:, None]
    same = (i // CHUNK) == (j // CHUNK)
    q, k = np.arange(P)[:, None], np.arange(P + CHUNK)[None, :]
    kpos = np.where(k < P, k, k - P - CHUNK)
    back = q // CHUNK - np.floor_divide(kpos, CHUNK)
    slopes = 2.0 ** (-8.0 * (np.arange(HB) + 1.0) / HB)
    alibi = np.where((back >= 0) & (back <= 1), -slopes[:, None, None] * np.abs(q - kpos)[None], NEG)
    return {
        "c_ident": np.eye(P, dtype=np.float32),
        "c_cums": np.stack([((j <= i) & same) / 16.0, ((j > i) & same) / 16.0], 1).astype(np.float32),
        "c_cind": (np.arange(P)[:, None] // CHUNK == np.arange(2)[None, :]).astype(np.float32) / 16.0,
        "c_causal": ((j <= i) & same).astype(np.int32),
        "c_alibi": np.ascontiguousarray(alibi.transpose(1, 0, 2)).astype(np.float32),
        "c_neghalf": np.full((P, HA), -0.5, np.float32),
        "c_rank": (j < i).astype(np.float32),
        "c_tie": np.tile(np.arange(EPG, 0, -1, dtype=np.float32), (P, 1)),
        "c_cols": np.tile(np.arange(NE, dtype=np.float32) * CAP, (P, 1)),
        "c_ovj": np.arange(NOV, dtype=np.float32)[None, :],
        "c_tok": (np.arange(NT)[None, :] * P + np.arange(P)[:, None]).astype(np.int32),
    }


def routing(nc, sem, bank, A, K, scratch, ctx):
    def sb(name, shape, dt=F32):
        return ctx.enter_context(nc.sbuf_tensor(name, shape, dt))

    rank_c = sb("rank_c", [P, P])
    ones = sb("ones", [P, P])
    tie = sb("tie", [P, EPG])
    cols = sb("cols", [P, NE])
    ovj = sb("ovj", [1, NOV])
    tok = sb("tok", [P, NT], I32)
    zero = sb("zero", [P, NSLOT // P], I32)
    gmax, wsum, gw = sb("gmax", [P, NT]), sb("wsum", [P, NT]), sb("gw", [P, NT])
    eg, ohg, pg = sb("eg", [P, NT, NG]), sb("ohg", [P, NT, NG]), sb("pg", [P, NT, NG])
    big = sb("big", [P, NT, NE])
    el, te = sb("el", [P, NT, EPG]), sb("te", [P, NT, EPG])
    oh = sb("oh", [P, 2, NT, EPG])
    mx = sb("mx", [P, 2, NT])
    OH = sb("OH", [P, 2, NT, NE])
    OHs, OHpre = sb("OHs", [P, NT, NE]), sb("OHpre", [P, NT, NE])
    tot, cnt, nov, cumov, base = (sb(n, [P, NE]) for n in ("tot", "cnt", "nov", "cumov", "base"))
    novi = sb("novi", [P, NE], I32)
    one_row = sb("one_row", [P, NE])
    rk, bm, bo, slot = (sb(n, [P, 2, NT]) for n in ("rk", "bm", "bo", "slot"))
    lo, hi, pos = (sb(n, [P, 2, NT], I32) for n in ("slot_lo", "slot_hi", "slot_pos"))
    ovc, meta_f = sb("ovc", [1, NOV, NE]), sb("meta_f", [1, NE + NOV + 1])
    logits, gates, dest, idx, meta = K["logits"], K["gates"], K["dest"], K["idx"], K["meta"]

    def sp_loads(sp):
        wait(sp, sem("logits_ready"), NT)
        sp.wait_ge(sem("v2_stored"), 16 * NT)
        for dst, src in ((rank_c[:, :], A["c_rank"]), (tie[:, :], A["c_tie"]), (cols[:, :], A["c_cols"]),
                         (ovj[:, :], A["c_ovj"]), (tok[:, :], A["c_tok"])):
            sp.dma_start(dst, src).then_inc(sem("route_consts"), 16)

    def sp_table(sp):
        sp.wait_ge(sem("zero_ready"), 1)
        sp.dma_start(scratch["table"].rearrange("(p c) o -> p (c o)", p=P), zero[:, :]).then_inc(sem("table_zeroed"), 16)

    def act_part(act):
        act.wait_ge(sem("route_args"), 1)
        act.activation(pg[:, :, :], eg[:, :, :], ACT.Exp).then_inc(sem("route_exps"), 1)
        act.wait_ge(sem("route_args"), 2)
        act.activation(mx[:, 1, :], mx[:, 1, :], ACT.Exp).then_inc(sem("route_exps"), 1)

    def pe_part(pe):
        pe.wait_ge(sem("onehots_ready"), 1)
        pe.wait_ge(sem("route_consts"), 5 * 16)
        flat = lambda t: t[:, :, :].rearrange("p t e -> p (t e)")
        pe.matmul(bank[0][:, :], rank_c[:, :], flat(OHs), start=True, stop=False)
        pe.matmul(bank[0][:, :], ones[:, :], flat(OHpre), start=False, stop=True)
        pe.matmul(bank[1][:, 0:NE], ones[:, :], tot[:, :], start=True, stop=True).then_inc(sem("ranks_done"), 1)

    def dve_part(v_):
        dve = nc.vector
        steps = [0]

        def link(ins):
            steps[0] += 1
            ins.then_inc(sem("route_steps"), 1)
            v_.wait_ge(sem("route_steps"), steps[0])

        v_.wait_ge(sem("route_consts"), 5 * 16)
        dve.memset(zero[:, :], 0).then_inc(sem("zero_ready"), 1)
        dve.memset(ones[:, :], 1.0)
        dve.memset(one_row[:, :], 1.0)
        dve.memset(OHpre[:, 0, :], 0.0)
        link(dve.tensor_reduce(gmax[:, :], logits[:, :, 0:NG], AX.X, ALU.max))
        link(dve.tensor_tensor(eg[:, :, :], logits[:, :, 0:NG], gmax[:, :].unsqueeze(2).to_broadcast([P, NT, NG]), ALU.subtract))

        def first_max(out, diff, tmp, m, n):
            link(dve.tensor_scalar(tmp, diff, 0.0, None, ALU.is_equal))
            link(dve.tensor_tensor(tmp, tmp, tie[:, None, EPG - n:EPG].to_broadcast([P, NT, n]), ALU.mult))
            link(dve.tensor_reduce(m, tmp, AX.X, ALU.max))
            link(dve.tensor_tensor(out, tmp, m.unsqueeze(2).to_broadcast([P, NT, n]), ALU.is_equal))

        dve.tensor_copy(wsum[:, :], gmax[:, :]).then_inc(sem("route_args"), 1)
        first_max(ohg[:, :, :], eg[:, :, :], te[:, :, 0:NG], gw[:, :], NG)
        v_.wait_ge(sem("route_exps"), 1)
        link(dve.tensor_reduce(wsum[:, :], pg[:, :, :], AX.X, ALU.add))
        link(dve.reciprocal(gw[:, :], wsum[:, :]))
        ohg_b = ohg[:, :, :].unsqueeze(3).to_broadcast([P, NT, NG, EPG])
        big4 = big[:, :, :].rearrange("p t (g e) -> p t g e", g=NG)
        link(dve.tensor_tensor(big4, logits[:, :, NG:NR].rearrange("p t (g e) -> p t g e", g=NG), ohg_b, ALU.mult))
        link(dve.tensor_reduce(el[:, :, :], big[:, :, :].rearrange("p t (g e) -> p t e g", g=NG), AX.X, ALU.add))
        for n in range(2):
            m = mx[:, n, :]
            link(dve.tensor_reduce(m, el[:, :, :], AX.X, ALU.max))
            link(dve.tensor_tensor(te[:, :, :], el[:, :, :], m.unsqueeze(2).to_broadcast([P, NT, EPG]), ALU.subtract))
            first_max(oh[:, n, :, :], te[:, :, :], te[:, :, :], gmax[:, :], EPG)
            if n == 0:
                link(dve.scalar_tensor_tensor(el[:, :, :], oh[:, 0, :, :], -3.0e38, el[:, :, :], ALU.mult, ALU.add))
        dve.tensor_tensor(mx[:, 1, :], mx[:, 1, :], mx[:, 0, :], ALU.subtract).then_inc(sem("route_args"), 1)
        v_.wait_ge(sem("route_exps"), 2)
        link(dve.tensor_scalar(gmax[:, :], mx[:, 1, :], 1.0, None, ALU.add))
        link(dve.reciprocal(gmax[:, :], gmax[:, :]))
        link(dve.tensor_tensor(gates[:, :, 0], gw[:, :], gmax[:, :], ALU.mult))
        link(dve.tensor_tensor(gates[:, :, 1], gates[:, :, 0], mx[:, 1, :], ALU.mult))
        for n in range(2):
            link(dve.tensor_tensor(OH[:, n, :, :].rearrange("p t (g e) -> p t g e", g=NG), ohg_b,
                                   oh[:, n, :, :].unsqueeze(2).to_broadcast([P, NT, NG, EPG]), ALU.mult))
        link(dve.tensor_tensor(OHs[:, :, :], OH[:, 0, :, :], OH[:, 1, :, :], ALU.add))
        for t in range(1, NT):
            link(dve.tensor_tensor(OHpre[:, t, :], OHpre[:, t - 1, :], OHs[:, t - 1, :], ALU.add))
        dve.tensor_tensor(tot[:, :], OHpre[:, NT - 1, :], OHs[:, NT - 1, :], ALU.add).then_inc(sem("onehots_ready"), 1)
        v_.wait_ge(sem("ranks_done"), 1)
        link(dve.tensor_copy(cnt[:, :], bank[1][:, 0:NE]))
        link(dve.tensor_scalar(novi[:, :], cnt[:, :], -1.0, 0.0, ALU.add, ALU.max))
        link(dve.tensor_single_scalar(novi[:, :], novi[:, :], 8, ALU.logical_shift_right))
        link(dve.tensor_copy(nov[:, :], novi[:, :]))
        link(dve.tensor_tensor_scan(cumov[:, :], one_row[:, :], nov[:, :], 0.0, ALU.mult, ALU.add))
        link(dve.tensor_tensor(base[:, :], cumov[:, :], nov[:, :], ALU.subtract))
        link(dve.tensor_scalar(base[:, :], base[:, :], float(CAP), float(NE * CAP - CAP), ALU.mult, ALU.add))
        for n in range(2):
            for dst, src in ((rk, bank[0][:, :].rearrange("p (t e) -> p t e", e=NE)),
                             (bm, cols[:, None, :].to_broadcast([P, NT, NE])),
                             (bo, base[:, None, :].to_broadcast([P, NT, NE]))):
                link(dve.tensor_tensor(big[:, :, :], OH[:, n, :, :], src, ALU.mult))
                link(dve.tensor_reduce(dst[:, n, :], big[:, :, :], AX.X, ALU.add))
        f = lambda t: t[:, :, :].rearrange("p a b -> p (a b)")
        link(dve.tensor_tensor(f(bo), f(bo), f(bm), ALU.subtract))
        link(dve.tensor_scalar(f(slot), f(rk), float(CAP), None, ALU.is_ge))
        link(dve.tensor_tensor(f(bo), f(bo), f(slot), ALU.mult))
        link(dve.tensor_tensor(f(bo), f(bo), f(bm), ALU.add))
        link(dve.tensor_tensor(f(slot), f(bo), f(rk), ALU.add))
        link(dve.tensor_copy(dest, f(slot)))
        link(dve.tensor_single_scalar(f(lo), dest, P - 1, ALU.bitwise_and))
        link(dve.tensor_single_scalar(f(hi), dest, 7, ALU.logical_shift_right))
        dve.scalar_tensor_tensor(f(pos), f(lo), float(NSLOT // P), f(hi), ALU.mult, ALU.add).then_inc(sem("slots_ready"), 1)
        row = meta_f[0:1, 0:NE]
        link(dve.tensor_scalar(row, cnt[0:1, :], float(WIDTHS[0]), None, ALU.is_gt))
        for w in WIDTHS[1:-1]:
            link(dve.scalar_tensor_tensor(row, cnt[0:1, :], float(w), row, ALU.is_gt, ALU.add))
        link(dve.tensor_tensor(ovc[:, :, :], cumov[0:1, None, :].to_broadcast([1, NOV, NE]),
                               ovj[:, :].unsqueeze(2).to_broadcast([1, NOV, NE]), ALU.is_le))
        link(dve.tensor_reduce(meta_f[0:1, NE:NE + NOV], ovc[:, :, :], AX.X, ALU.add))
        link(dve.tensor_scalar(meta_f[0:1, NE:NE + NOV], meta_f[0:1, NE:NE + NOV], float(NE - 1), None, ALU.min))
        link(dve.tensor_copy(meta_f[0:1, NE + NOV:NE + NOV + 1], cumov[0:1, NE - 1:NE]))
        dve.tensor_copy(meta[0:1, 0:NE + NOV + 1], meta_f[0:1, :]).then_inc(sem("meta_ready"), 1)

    def pool_part(po):
        po.wait_ge(sem("slots_ready"), 1)
        po.wait_ge(sem("table_zeroed"), 16)
        for t in range(NT):
            for n in range(2):
                po.indirect_dma_start(out=scratch["table"], in_=tok[:, t:t + 1],
                                      out_offset=bass.IndirectOffsetOnAxis(ap=pos[:, n, t:t + 1], axis=0),
                                      in_offset=None).then_inc(sem("table_filled"), 16)
        po.wait_ge(sem("table_filled"), 16 * 2 * NT)
        po.dma_start(idx, scratch["table"].rearrange("(p c) o -> p (c o)", p=P)).then_inc(sem("idx_loaded"), 16)
        po.wait_ge(sem("idx_loaded"), 16)

    return sp_loads, sp_table, pe_part, act_part, dve_part, pool_part


def experts(nc, sem, bank, A, K, scratch, W, ctx):
    def sb(name, shape, dt=F32):
        return ctx.enter_context(nc.sbuf_tensor(name, shape, dt))

    xg = sb("xg", [P, 2, 2, D])
    xT = sb("xT", [P, 2, KD, CAP])
    sg = sb("sg", [P, KF, CAP])
    hT = sb("hT", [P, KF, CAP])
    yT = sb("yT", [P, KD, CAP])
    y = sb("y", [P, 2, 2, D])
    idxc = sb("idxc", [P, 2, 2], I32)
    ident, norm2, meta, idx = K["ident"], K["norm2"], K["meta"], K["idx"]
    wg, wu, wd = W
    meta_rider = (sem("meta_ready"), 1)
    GU, DN, XB, YB = bank[0:2], bank[2:4], bank[4:6], bank[6:8]

    def after(eng, pre, name, n):
        eng.wait_ge(sem(pre + name), n + CREDIT)

    def credit(eng, *names):
        for pre in ("m_", "o_"):
            for name in names:
                eng.sem_inc(sem(pre + name), CREDIT)

    def load(sp, pre, which, q, e):
        dst, name = {"g": (wg, "w_gate"), "u": (wu, "w_up"), "d": (wd, "w_down")}[which]
        src = A[name][0, e:e + 1] if isinstance(e, int) else A[name][0, bass.ds(e, 1)]
        sp.dma_start(dst[:, q, :, :], src.rearrange("e (k p) n -> p (e k) n", p=P)).then_inc(sem(f"{pre}{name}_loaded{q}"), 16)

    def store(sp, pre, q, rest, row):
        def rows(lo, n):
            return scratch["y"][row + lo:row + lo + n, :] if isinstance(row, int) else scratch["y"][bass.ds(row + lo, n), :]
        sp.dma_start(rows(0, P), y[:, q, 0, :]).then_inc(sem(f"{pre}y_stored{q}"), 16)
        if rest:
            sp.dma_start(rows(P, rest), y[0:rest, q, 1, :]).then_inc(sem(f"{pre}y_stored{q}"), 16)
        else:
            sp.sem_inc(sem(f"{pre}y_stored{q}"), 16)

    def clear_xg(v_):
        v_.wait_ge(sem("table_filled"), 16 * 2 * NT)
        nc.vector.memset(xg[:, :, 1, :], 0.0).then_inc(sem("xg_cleared"), 1)

    def gather(po, pre, n, q, rest, col):
        for part, rows in ((0, P), (1, rest)):
            po.indirect_dma_start(out=xg[0:rows, q, part, :], in_=scratch["v2"], out_offset=None,
                                  in_offset=bass.IndirectOffsetOnAxis(ap=idxc[0:rows, q, part:part + 1], axis=0))\
                .then_inc(sem(f"{pre}xg_loaded{q}"), 16)

    def copy_index(po, pre, n, q, col):
        wait_apart(po, meta_rider, (sem(pre + "x_done"), 4 * (n - 1) + CREDIT))
        nc.gpsimd.tensor_copy(idxc[:, q, :], idx[:, bass.ds(col, 2)] if not isinstance(col, int) else idx[:, col:col + 2])\
            .then_inc(sem(pre + "index_ready"), 1)
        wait_apart(po, meta_rider, (sem(pre + "index_ready"), n + 1))

    def pe_x(pe, pre, n, q, steps):
        for j in steps:
            if j == 0:
                wait(pe, sem(f"{pre}xg_loaded{q}"), 32 * K["lap"](pre, n, q))
            after(pe, pre, "xT_ready", 4 * n + j - 1)
            for kk in range(2):
                c = slice((2 * j + kk) * P, (2 * j + kk + 1) * P)
                for part in range(2):
                    m = pe.transpose(XB[j % 2][:, kk * CAP + part * P:kk * CAP + (part + 1) * P], xg[:, q, part, c], ident)
            m.then_inc(sem(pre + "x_done"), 1)

    def pe_gu(pe, pre, n, q, w):
        for m_ in range(KF):
            if m_ == 0:
                after(pe, pre, "xT_ready", 4 * n + 4)
                wait(pe, sem(f"{pre}w_gate_loaded{q}"), 16 * K["lap"](pre, n, q))
                wait(pe, sem(f"{pre}w_up_loaded{q}"), 16 * K["lap"](pre, n, q))
            after(pe, pre, "h_ready", 4 * n + m_ - 1)
            for half, wt in enumerate((wg, wu)):
                for k in range(KD):
                    m = pe.matmul(GU[m_ % 2][:, half * CAP:half * CAP + w], wt[:, q, k, m_ * P:(m_ + 1) * P],
                                  xT[:, q, k, 0:w], start=k == 0, stop=k == KD - 1)
            m.then_inc(sem(pre + "g_done"), 1)

    def pe_down(pe, pre, n, q, w):
        for j in range(4):
            if j == 0:
                after(pe, pre, "h_ready", 4 * n + 4)
                wait(pe, sem(f"{pre}w_down_loaded{q}"), 16 * K["lap"](pre, n, q))
            after(pe, pre, "yT_ready", 4 * n + j - 1)
            for mm in range(2):
                c = slice((2 * j + mm) * P, (2 * j + mm + 1) * P)
                for k in range(KF):
                    m = pe.matmul(DN[j % 2][:, mm * CAP:mm * CAP + w], wd[:, q, k, c], hT[:, k, 0:w],
                                  start=k == 0, stop=k == KF - 1)
            m.then_inc(sem(pre + "d_done"), 1)

    def pe_y(pe, pre, n, w):
        for part in range(2 if w > P else 1):
            for half in range(2):
                after(pe, pre, "yT_ready", 4 * n + 2 * half + 2)
                after(pe, pre, ("yA_taken", "yD_taken")[half], 2 * n + part)
                for mm in range(4):
                    m = pe.transpose(YB[half][:, mm * P:(mm + 1) * P], yT[:, 4 * half + mm, part * P:(part + 1) * P], ident)
                m.then_inc(sem(pre + "yb_done"), 3 if w <= P and half == 1 else 1)

    def pe_chunk(pe, pre, n, q, w, next_x):
        pe_gu(pe, pre, n, q, w)
        next_x((0, 1))
        pe_down(pe, pre, n, q, w)
        next_x((2, 3))
        pe_y(pe, pre, n, w)

    def act_chunk(act, pre, n, q):
        for m_ in range(KF):
            after(act, pre, "g_done", 4 * n + m_ + 1)
            after(act, pre, "h_ready", 4 * (n - 1) + m_ + 1)
            act.activation(sg[:, m_, :], GU[m_ % 2][:, 0:CAP], ACT.Silu).then_inc(sem(pre + "sg_ready"), 1)
        for j in range(4):
            after(act, pre, "d_done", 4 * n + j + 1)
            after(act, pre, "yb_done", 4 * n)
            act.activation(yT[:, 2 * j:2 * j + 2, :], DN[j % 2][:, :].rearrange("p (a b) -> p a b", a=2),
                           ACT.Copy).then_inc(sem(pre + "yT_ready"), 1)
        wait(act, sem(f"{pre}y_stored{q}"), 32 * K["lap"](pre, n, q))
        for part in range(2):
            after(act, pre, "yb_done", 4 * n + 2 * part + 1)
            act.activation(y[:, q, part, 0:512], YB[0][:, :], ACT.Copy).then_inc(sem(pre + "yA_taken"), 1)

    def dve_x(v_, pre, n, q):
        for j in range(4):
            after(v_, pre, "x_done", 4 * n + j + 1)
            after(v_, pre, "g_done", 4 * (n - 1))
            nc.vector.tensor_tensor(xT[:, q, 2 * j:2 * j + 2, :], XB[j % 2][:, :].rearrange("p (a b) -> p a b", a=2),
                                    norm2[:, 2 * j:2 * j + 2].unsqueeze(2).to_broadcast([P, 2, CAP]), ALU.mult)\
                .then_inc(sem(pre + "xT_ready"), 1)

    def dve_h(v_, pre, n, q):
        for m_ in range(KF):
            after(v_, pre, "sg_ready", 4 * n + m_ + 1)
            after(v_, pre, "d_done", 4 * n)
            nc.vector.tensor_tensor(hT[:, m_, :], GU[m_ % 2][:, CAP:2 * CAP], sg[:, m_, :], ALU.mult)\
                .then_inc(sem(pre + "h_ready"), 1)

    def dve_y(v_, pre, n, q):
        wait(v_, sem(f"{pre}y_stored{q}"), 32 * K["lap"](pre, n, q))
        for part in range(2):
            after(v_, pre, "yb_done", 4 * n + 2 * part + 2)
            nc.vector.tensor_copy(y[:, q, part, 512:D], YB[1][:, :]).then_inc(sem(pre + "yD_taken"), 1)

    return credit, load, store, clear_xg, gather, copy_index, pe_x, pe_chunk, act_chunk, dve_x, dve_h, dve_y


def by_width(eng, cls, body, of=lambda w: w):
    def among(lo, hi):
        kinds = {of(w) for w in WIDTHS[lo:hi]}
        if len(kinds) == 1:
            body(kinds.pop())
            return
        mid = (lo + hi) // 2
        with eng.If(cls < mid):
            among(lo, mid)
        with eng.Else():
            among(mid, hi)
    among(0, len(WIDTHS))


def rest_stored(w):
    return max(w - P, 0)


def rest_gathered(w):
    return max(w - P, 16)


NYG = 4


def combine(nc, sem, A, K, scratch, W, ctx):
    def sb(name, shape, dt=F32):
        return ctx.enter_context(nc.sbuf_tensor(name, shape, dt))

    wgu, wd = W[0], W[1]
    hc = wgu[:, :, :, :, :].rearrange("p w q k n -> p (w q k n)").rearrange("p (t d) -> p t d", d=D)
    yg = wd[:, :, :, :].rearrange("p q k n -> p (q k) n").rearrange("p (b n) d -> p b n d", b=NYG)
    oc = sb("oc", [P, 2, D])
    fw = sb("fw", [P, D])
    fjunk = sb("fjunk", [P, 2, D], BF16)
    dc = sb("dc", [P, NYG, 2], I32)
    gc = sb("gc", [P, NYG, 2])
    fs = sb("fs", [P, NYG, 2])
    nh = sb("nh", [P, HA])
    gates, dest = K["gates"], K["dest"]
    rider = (sem("meta_ready"), 1)
    TPQ = NT // 4

    def tile(ap, t):
        return ap[:, t, :] if isinstance(t, int) else ap[:, bass.ds(t, 1), :].rearrange("p o n -> p (o n)")

    def sp_first(sp):
        sp.dma_start(fw[:, :], A["final_norm_w"].rearrange("(o n) -> o n", o=1).to_broadcast([P, D])).then_inc(sem("fw_loaded"), 16)
        sp.dma_start(nh[:, :], A["c_neghalf"]).then_inc(sem("fw_loaded"), 16)

    def sp_h(sp, q):
        for n in range(2):
            t0 = (2 * n + q) * TPQ
            sp.dma_start(hc[:, t0:t0 + TPQ, :], scratch["h"][t0 * P:(t0 + TPQ) * P, :].rearrange("(t p) d -> p t d", p=P))\
                .then_inc(sem("h_back"), 16)

    def sp_tile(sp, group, n):
        t, q = NYG * group + n, n % 2
        wait_apart(sp, rider, (sem("sum_o_ready"), t + 1))
        dst = A["out"][t * P:(t + 1) * P, :] if isinstance(t, int) else A["out"][bass.ds(t * P, P), :]
        sp.dma_start(dst, oc[:, q, :]).then_inc(sem(f"out_stored{q}"), 16)

    def pool_gather(po, t, b):
        wait_apart(po, rider, (sem("sum_s_ready"), t - NYG + 1 + NYG))
        d = dest.rearrange("p (n t) -> p n t", n=2)
        nc.gpsimd.tensor_copy(dc[:, b, :], d[:, :, t] if isinstance(t, int) else d[:, :, bass.ds(t, 1)].rearrange("p n o -> p (n o)"))\
            .then_inc(sem("sum_dc_ready"), 1)
        wait_apart(po, rider, (sem("sum_dc_ready"), t + 1))
        for n in range(2):
            po.indirect_dma_start(out=yg[:, b, n, :], in_=scratch["y"], out_offset=None,
                                  in_offset=bass.IndirectOffsetOnAxis(ap=dc[:, b, n:n + 1], axis=0)).then_inc(sem(f"yg_loaded{b}"), 16)

    def pool_tile(po, group, n):
        t = NYG * group + n
        if not isinstance(t, int) or t + 2 < NT:
            pool_gather(po, t + 2, (n + 2) % NYG)
        wait_apart(po, rider, (sem("fss_ready"), t + 1))
        nc.gpsimd.tensor_scalar(fs[:, n, 0:1], fs[:, n, 0:1], 1.0 / D, EPS, ALU.mult, ALU.add).then_inc(sem("fmean"), 1)
        wait_apart(po, rider, (sem("fmean"), t + 1))
        nc.gpsimd.tensor_tensor(fs[:, n, 1:2], fs[:, n, 0:1], nh[:, 0:1], ALU.pow).then_inc(sem("froot_ready"), 1)

    def act_tile(act, group, n):
        t = NYG * group + n
        wait(act, sem("sum_s_ready"), t + 1 + NYG)
        act.activation(fjunk[:, n % 2, :], tile(hc, t), ACT.Square, accum_out=fs[:, n, 0:1]).then_inc(sem("fss_ready"), 1)

    def dve_sum(v_, group, n):
        t = NYG * group + n
        nc.vector.tensor_copy(gc[:, n, :], tile(gates, t)).then_inc(sem("sum_steps"), 1)
        v_.wait_ge(sem("sum_steps"), 2 * t + 1)
        v_.wait_ge(sem(f"yg_loaded{n}"), 32 * (group + 1))
        ht = tile(hc, t)
        nc.vector.scalar_tensor_tensor(ht, yg[:, n, 0, :], gc[:, n, 0:1], ht, ALU.mult, ALU.add).then_inc(sem("sum_steps"), 1)
        v_.wait_ge(sem("sum_steps"), 2 * t + 2)
        nc.vector.scalar_tensor_tensor(ht, yg[:, n, 1, :], gc[:, n, 1:2], ht, ALU.mult, ALU.add).then_inc(sem("sum_s_ready"), 1)

    def dve_tile(v_, group, n):
        t, q = NYG * group + n, n % 2
        if not isinstance(t, int) or t + 1 < NT:
            dve_sum(v_, group + (n + 1) // NYG, (n + 1) % NYG)
        v_.wait_ge(sem("froot_ready"), t + 1)
        v_.wait_ge(sem(f"out_stored{q}"), 16 * (2 * group + n // 2) + 16)
        nc.vector.scalar_tensor_tensor(oc[:, q, :], tile(hc, t), fs[:, n, 1:2], fw[:, :], ALU.mult, ALU.mult).then_inc(sem("sum_o_ready"), 1)

    return sp_first, sp_h, sp_tile, pool_gather, pool_tile, act_tile, dve_sum, dve_tile


def tile_groups(eng, step):
    with eng.Fori(0, NT // NYG - 1) as group:
        for n in range(NYG):
            step(eng, group, n)
    for n in range(NYG):
        step(eng, NT // NYG - 1, n)


def program(nc, A):
    with ExitStack() as ctx:
        sem = Semaphores(nc, ctx)
        bank = [ctx.enter_context(nc.psum_tensor(f"bank{n}", [P, 512], F32)) for n in range(8)]

        def sb(name, shape, dt=F32):
            return ctx.enter_context(nc.sbuf_tensor(name, shape, dt))

        ident, norm2, logits = sb("ident", [P, P]), sb("norm2_sb", [P, KD]), sb("logits", [P, NT, NR])
        gates, dest = sb("gates", [P, NT, 2]), sb("dest", [P, 2 * NT], I32)
        idx, meta = sb("idx", [P, NSLOT // P], I32), sb("meta", [1, 64], I32)
        K = {"ident": ident[:, :], "norm2": norm2[:, :], "logits": logits, "gates": gates, "dest": dest[:, :],
             "idx": idx[:, :], "meta": meta,
             "lap": lambda pre, n, q: (n + 1) if pre == "o_" else ((n - q) // 2 + 1 if isinstance(n, int) else K["pair"] + 1)}
        scratch = {"h": nc.dram_tensor("h_dram", (SEQ, D), F32).ap(), "v2": nc.dram_tensor("v2_dram", (SEQ, D), F32).ap(),
                   "y": nc.dram_tensor("y_dram", (NSLOT, D), F32).ap(),
                   "table": nc.dram_tensor("table_dram", (NSLOT, 1), I32).ap()}
        with ExitStack() as mem:
            mix_sp_loads, mix_sp, mix_pe, mix_act, mix_dve, mix_pool = mixer(nc, sem, bank, A, K, scratch, mem)
        wgu = ctx.enter_context(nc.sbuf_tensor("wgu", [P, 2, 2, KD, FF], F32))
        wd = ctx.enter_context(nc.sbuf_tensor("wd", [P, 2, KF, D], F32))
        cb_sp_first, cb_sp_h, cb_sp, cb_gather, cb_pool, cb_act, cb_sum, cb_dve = combine(nc, sem, A, K, scratch, (wgu, wd), ctx)
        with ExitStack() as mem:
            rt_sp_loads, rt_sp_table, rt_pe, rt_act, rt_dve, rt_pool = routing(nc, sem, bank, A, K, scratch, mem)
        with ExitStack() as mem:
            (credit, load, store, clear_xg, gather, copy_index, pe_x, pe_chunk, act_chunk, dve_x, dve_h, dve_y) = \
                experts(nc, sem, bank, A, K, scratch, (wgu[:, 0], wgu[:, 1], wd), mem)
        block = ctx.enter_context(nc.Block())

        def chunk_class(eng, e):
            return eng.value_load(meta[0:1, e:e + 1] if isinstance(e, int) else meta[0:1, bass.ds(e, 1)],
                                  min_val=0, max_val=len(WIDTHS) - 1)

        def lap_is(pair):
            K["pair"] = pair

        def overflow(eng, body, last=None):
            n_over = eng.value_load(meta[0:1, NE + NOV:NE + NOV + 1], min_val=0, max_val=NOV)
            with eng.If(n_over > 0):
                for q in range(2):
                    eng.wait_ge(sem(f"m_y_stored{q}"), 16 * NE + 32)
                eng.nop()
                with eng.Fori(0, NOV) as j:
                    with eng.If(j < n_over):
                        body(j)
                if last:
                    last()
                eng.nop()

        @block.sync
        def _(sp):
            sp.wait_ge(sem("filled"), 1)
            mix_sp_loads(sp)
            for q in range(2):
                sp.sem_inc(sem(f"m_y_stored{q}"), 32)
                sp.sem_inc(sem(f"out_stored{q}"), 16)
            sp.sem_inc(sem("o_y_stored0"), 32)
            mix_sp(sp, 0, 0)
            mix_sp(sp, 1, 1)
            with sp.Fori(1, NT // 2) as pair:
                mix_sp(sp, 2 * pair, 0)
                mix_sp(sp, 2 * pair + 1, 1)
            sp.wait_ge(sem("qb_done"), NT)
            load(sp, "m_", "g", 0, 0)
            mix_sp(sp, NT, 0)
            mix_sp(sp, NT + 1, 1)
            rt_sp_loads(sp)
            rt_sp_table(sp)
            cb_sp_first(sp)
            sp.wait_ge(sem("wo_done"), 2 * NT)
            load(sp, "m_", "u", 0, 0)
            load(sp, "m_", "d", 0, 0)
            for which in "gud":
                load(sp, "m_", which, 1, 1)
            sp.wait_ge(sem("meta_ready"), 1)
            sp.wait_ge(sem("y_cleared"), 16 * NE * 2)

            def expert(pair, q):
                lap_is(pair)
                e = 2 * pair + q
                cls = chunk_class(sp, e)
                more = not isinstance(e, int)
                wait_apart(sp, (sem("meta_ready"), 1), (sem("m_g_done"), 4 * e + 4 + CREDIT))
                if more:
                    load(sp, "m_", "g", q, e + 2)
                    load(sp, "m_", "u", q, e + 2)
                    wait_apart(sp, (sem("meta_ready"), 1), (sem("m_d_done"), 4 * e + 4 + CREDIT))
                    load(sp, "m_", "d", q, e + 2)
                else:
                    cb_sp_h(sp, q)
                wait_apart(sp, (sem("meta_ready"), 1), (sem("m_yA_taken"), 2 * e + 2 + CREDIT), (sem("m_yD_taken"), 2 * e + 2 + CREDIT))
                by_width(sp, cls, lambda rest: store(sp, "m_", q, rest, e * CAP), rest_stored)

            with sp.Fori(0, NE // 2 - 1) as pair:
                for q in range(2):
                    expert(pair, q)
            for q in range(2):
                expert(NE // 2 - 1, q)

            def over(j):
                e = sp.value_load(meta[0:1, bass.ds(NE + j, 1)], min_val=0, max_val=NE - 1)
                wait_apart(sp, (sem("h_back"), 4 * 16), (sem("o_d_done"), 4 * j + CREDIT))
                for which in "gud":
                    load(sp, "o_", which, 0, e)
                wait_apart(sp, (sem("meta_ready"), 1), (sem("o_yA_taken"), 2 * j + 2 + CREDIT), (sem("o_yD_taken"), 2 * j + 2 + CREDIT))
                store(sp, "o_", 0, CAP - P, (NE + j) * CAP)

            def h_again():
                cb_sp_h(sp, 0)
                sp.wait_ge(sem("h_back"), 6 * 16)
            overflow(sp, over, h_again)
            sp.wait_ge(sem("h_back"), 4 * 16)
            for q in range(2):
                sp.wait_ge(sem(f"m_y_stored{q}"), 16 * NE + 32)
            sp.sem_inc(sem("h_there"), 1)
            tile_groups(sp, cb_sp)
            for q in range(2):
                sp.wait_ge(sem(f"out_stored{q}"), 16 * (NT // 2 + 1))

        @block.tensor
        def _(pe):
            credit(pe, "x_done", "g_done", "d_done", "yb_done")
            pe.wait_ge(sem("first_consts"), 4 * 16)
            pipeline(pe, mix_pe)
            rt_pe(pe)
            pe.wait_ge(sem("meta_ready"), 1)
            pe_x(pe, "m_", 0, 0, range(4))
            with pe.Fori(0, NE // 2) as pair:
                for q in range(2):
                    e = 2 * pair + q

                    def next_x(steps):
                        lap_is(pair + q)
                        pe_x(pe, "m_", e + 1, 1 - q, steps)
                        lap_is(pair)

                    lap_is(pair)
                    by_width(pe, chunk_class(pe, e), lambda w: pe_chunk(pe, "m_", e, q, w, next_x))

            def over(j):
                pe_x(pe, "o_", j, 0, range(4))
                pe_chunk(pe, "o_", j, 0, CAP, lambda steps: None)
            overflow(pe, over)

        @block.scalar
        def _(act):
            credit(act, "sg_ready", "yT_ready", "yA_taken")
            pipeline(act, mix_act)
            rt_act(act)
            act.wait_ge(sem("meta_ready"), 1)
            with act.Fori(0, NE // 2) as pair:
                lap_is(pair)
                for q in range(2):
                    act_chunk(act, "m_", 2 * pair + q, q)
            overflow(act, lambda j: act_chunk(act, "o_", j, 0))
            tile_groups(act, cb_act)

        @block.vector
        def _(v_):
            credit(v_, "xT_ready", "h_ready", "yD_taken")
            v_.sem_inc(sem("sum_s_ready"), NYG)
            pipeline(v_, mix_dve)
            rt_dve(v_)
            v_.wait_ge(sem("meta_ready"), 1)
            clear_xg(v_)
            dve_x(v_, "m_", 0, 0)
            with v_.Fori(0, NE // 2) as pair:
                for q in range(2):
                    e = 2 * pair + q
                    lap_is(pair)
                    dve_h(v_, "m_", e, q)
                    dve_x(v_, "m_", e + 1, 1 - q)
                    dve_y(v_, "m_", e, q)

            def over(j):
                dve_x(v_, "o_", j, 0)
                dve_h(v_, "o_", j, 0)
                dve_y(v_, "o_", j, 0)
            overflow(v_, over)
            v_.wait_ge(sem("fw_loaded"), 32)
            v_.wait_ge(sem("h_there"), 1)
            cb_sum(v_, 0, 0)
            tile_groups(v_, cb_dve)

        @block.gpsimd
        def _(po):
            pipeline(po, mix_pool)
            rt_pool(po)
            po.wait_ge(sem("meta_ready"), 1)
            po.wait_ge(sem("xg_cleared"), 1)
            with po.Fori(0, NE // 2) as pair:
                lap_is(pair)
                for q in range(2):
                    e = 2 * pair + q
                    cls = chunk_class(po, e)
                    copy_index(po, "m_", e, q, 2 * e)
                    by_width(po, cls, lambda rest: gather(po, "m_", e, q, rest, 2 * e), rest_gathered)
            copy_index(po, "m_", NE, 0, 0)
            gather(po, "m_", NE, 0, rest_gathered(0), 0)

            def over(j):
                copy_index(po, "o_", j, 0, 2 * (NE + j))
                gather(po, "o_", j, 0, CAP - P, 0)
                wait_apart(po, (sem("meta_ready"), 1), (sem("o_y_stored0"), 32 * j + 64))
                po.nop()
            overflow(po, over)
            for q in range(2):
                po.wait_ge(sem(f"m_y_stored{q}"), 16 * NE + 32)
            po.wait_ge(sem("m_x_done"), 4 * NE + 4 + CREDIT)
            po.wait_ge(sem("m_xT_ready"), 4 * NE + 4 + CREDIT)
            po.wait_ge(sem("fw_loaded"), 32)
            po.wait_ge(sem("h_there"), 1)
            cb_gather(po, 0, 0)
            cb_gather(po, 1, 1)
            tile_groups(po, cb_pool)


def kernel(**inputs):
    import concourse.bacc as bacc
    from concourse.bass_utils import run_bass_kernel_spmd

    a = {k: np.ascontiguousarray(v) for k, v in inputs.items()}
    a["x"] = a["x"].reshape(SEQ, D)
    a["norm1_t"] = np.ascontiguousarray(a.pop("norm1_w").reshape(KD, P).T)
    a["norm2_t"] = np.ascontiguousarray(a.pop("norm2_w").reshape(KD, P).T)
    b = a["b_in"][0]
    lr = np.zeros(P, b.dtype)
    lr[:LOWRANK] = b[C_LR:C_QB]
    a["b_fm"] = np.ascontiguousarray(np.stack([b[C_QB + n * P:C_QB + (n + 1) * P] for n in range(5)] + [lr], 1))
    a["w_a2"] = np.concatenate([a.pop("gla_w_a2")[0], a.pop("gla_b_a2")], 0)
    a.update(host_constants())
    nc = bacc.Bacc("TRN2", target_bir_lowering=False, num_devices=1)
    A = {k: nc.dram_tensor(k + "_in", v.shape, mybir.dt.from_np(v.dtype), kind="ExternalInput").ap() for k, v in a.items()}
    A["out"] = nc.dram_tensor("out", (SEQ, D), F32, kind="ExternalOutput").ap()
    program(nc, A)
    r = run_bass_kernel_spmd(nc, [{k + "_in": v for k, v in a.items()}], core_ids=[0])
    return r.results[0]["out"].reshape(1, SEQ, D)
```

```python
from contextlib import ExitStack

import concourse.bass as bass
import numpy as np
from concourse import mybir

F32 = mybir.dt.float32
BF16 = mybir.dt.bfloat16
I32 = mybir.dt.int32
ALU = mybir.AluOpType
ACT = mybir.ActivationFunctionType
AX = mybir.AxisListType

P = 128
SEQ, D = 2048, 1024
NT = SEQ // P
KD = D // P
CHUNK = 64
EPS = 1e-6
HA, DK, DV, LOWRANK = 4, 64, 128, 16
HB, HD = 8, 64
WK = P + CHUNK
QKA, VA = HA * DK, HA * DV
NEG = -1.0e30
C_QK, C_V, C_G, C_LR, C_QB = 0, 2 * QKA, 2 * QKA + VA, 2 * QKA + 2 * VA, 2 * QKA + 2 * VA + LOWRANK
C_KB = C_QB + HB * HD
C_VB = C_KB + 2 * HD
IN_W = C_VB + 2 * HD
S_QB, S_KB, S_VB, S_LR = C_LR, C_LR + HB * HD, C_LR + HB * HD + 2 * HD, IN_W - LOWRANK
NG, EPG = 4, 8
NE = NG * EPG
NR = NG + NE
FF = 512
KF = FF // P
CAP = 256
NOV = 16
NSLOT = (NE + NOV) * CAP
WIDTHS = (128, 136, 144, 152, 160, 176, 208, 256)


def wait(eng, sem, n):
    if not (isinstance(n, int) and n <= 0):
        eng.wait_ge(sem, n)


def wait_apart(eng, rider, *waits):
    waits = [(sem, n if isinstance(n, int) else eng.compute_val(n)) for sem, n in waits
             if not (isinstance(n, int) and n <= 0)]
    eng.wait_ge(*rider)
    for sem, n in waits:
        eng.wait_ge(sem, n)


CREDIT = 16


class Semaphores:

    def __init__(self, nc, ctx):
        self.made, self.nc, self.ctx = {}, nc, ctx

    def __call__(self, name):
        if name not in self.made:
            self.made[name] = self.ctx.enter_context(self.nc.semaphore(name))
        return self.made[name]


JOBS = [
    ("qk", 0, {"qk_ready": (1, 1)}), ("qdki", 1, {"qdkiT_ready": (1, 1)}),
    ("u2Ta", 2, {"u2T_ready": (2, 1)}), ("u2Tb", 2, {"u2T_ready": (2, 2)}),
    ("att0", 1, {"att_ready": (2, 1)}), ("att1", 1, {"att_ready": (2, 2)}),
    ("dS0", 1, {"Smid_ready": (1, 1)}),
    ("dS1", 1, {"S_ready": (1, 1)}), ("v", 0, {"v_ready": (1, 1)}),
    ("router", 2, {"logits_ready": (1, 1)}),
    ("pTp", 1, {"pT_ready": (3, 1)}), ("pTc0", 1, {"pT_ready": (3, 2)}),
    ("pTc1", 1, {"pT_ready": (3, 3)}), ("g", 0, {"g_ready": (1, 1)}),
    ("og0", 1, {"og_taken": (2, 1)}), ("og1", 1, {"og_taken": (2, 2)}),
    ("ob0", 1, {"ob_taken": (2, 1)}), ("ob1", 1, {"ob_taken": (2, 2)}),
    ("kv", 0, {"kb_taken": (1, 1), "vb_ready": (1, 1)}), ("mixAT", 1, {"mixAT_taken": (1, 1)}),
    ("la", 0, {"ls_ready": (1, 1)}), ("qb", 0, {"qbT_ready": (1, 1)}),
    ("xTa", -1, {"uT_ready": (2, 1)}), ("xTb", -1, {"uT_ready": (2, 2)}),
    ("wo0", 1, {"h_ready": (2, 1)}), ("wo1", 1, {"h_ready": (2, 2)}),
    ("s0", 0, {"s_taken": (4, 1)}), ("s1", 0, {"s_taken": (4, 2)}),
    ("s2", 0, {"s_taken": (4, 3)}), ("s3", 0, {"s_taken": (4, 4)}),
    ("bb", 0, {"decays_ready": (1, 1)}), ("bl", 0, {"dec_ready": (1, 1)}),
]
INDEX = {name: k for k, (name, _, _) in enumerate(JOBS)}


def mixer(nc, sem, bank, A, C, scratch, ctx):
    def sb(name, shape, dt=F32):
        return ctx.enter_context(nc.sbuf_tensor(name, shape, dt))

    w_in = sb("w_in_sb", [P, KD, IN_W])
    w_out = sb("w_out_sb", [P, KD, D])
    b_tm = sb("b_tm", [P, C_LR + 2 * HD + LOWRANK])
    b_fm = sb("b_fm", [P, 5])
    norm1 = sb("norm1_sb", [P, KD])
    gnorm = sb("gnorm_sb", [P, DV])
    w_a2 = sb("w_a2_sb", [LOWRANK + 1, QKA])
    sinks = sb("sinks_sb", [P, HB])
    w_r = sb("w_r_sb", [P, KD, NR])
    b_r = sb("b_r_sb", [P, NR])
    alibi = sb("alibi", [P, HB, WK])
    cums = sb("cums", [P, 2, P])
    cind = sb("cind", [P, 2])
    causal = sb("causal", [P, P], I32)
    neghalf = sb("neghalf", [P, HA])

    x = sb("x_sb", [P, D])
    h = sb("h_sb", [P, 2, D])
    xn = sb("xn", [P, D])
    v2 = sb("v2_sb", [P, D])
    junk = sb("junk", [P, D], BF16)
    uT = sb("uT", [P, KD, P])
    u2T = sb("u2T", [P, KD, P])
    ss = sb("ss", [P, 16])
    qk = sb("qk_sb", [P, 2 * QKA])
    v = sb("v_sb", [P, 2, VA])
    g = sb("g_sb", [P, VA])
    gm = sb("gm", [P, VA])
    lrT = sb("lrT", [LOWRANK + 1, P])
    la_t = sb("la_t", [P, QKA])
    g_t = sb("g_t", [P, VA])
    ls = sb("ls_sb", [P, QKA])
    E = sb("decays", [P, 3, QKA])
    dec = sb("dec", [P, 4])
    qd = sb("qd", [P, QKA])
    ki = sb("ki", [P, QKA])
    ke = sb("ke", [P, QKA])
    qdkiT = sb("qdkiT", [P, 4, P])
    attm = sb("attm", [P, HA, P])
    S = sb("S", [P, 2, 2, DV])
    Smid = sb("Smid", [P, 2, DV])
    mixA = sb("mixA", [P, VA])
    mixT = sb("mixT", [P, KD, P])
    qbT = sb("qbT", [P, 4, P])
    kb = sb("kb_sb", [P, 2, WK])
    vb = sb("vb_sb", [P, 2, 2 * HD + LOWRANK])
    vlo = sb("vlo", [CHUNK, 2 * HD])
    sc = sb("sc", [P, HB, WK])
    pp = g_t[:, :].rearrange("p (h j) -> p h j", h=HB)
    sm = sb("sm", [P, 6, HB])
    pTp = sb("pTp", [P, 4, P])
    pTc = sb("pTc", [P, HB, P])
    nought = sb("nought", [P, 128])
    ident, norm2, logits = C["ident"], C["norm2"], C["logits"]
    m_, nm, sums, esink, den, rden = (sm[:, n, :] for n in range(6))

    b_tm_vb = b_tm[:, C_LR:C_LR + 2 * HD + LOWRANK]

    def loads(sp):
        sp.dma_start(x[:, :], A["x"][0:P, :]).then_inc(sem("x_loaded"), 16)
        first = [(ident, A["c_ident"]), (norm1[:, :], A["norm1_t"]), (norm2, A["norm2_t"]),
                 (C["tie"][:, :], A["c_tie"]),
                 (neghalf[:, :], A["c_neghalf"])]
        for dst, src in first:
            sp.dma_start(dst, src).then_inc(sem("first_consts"), 16)
        for lo, hi in ((0, C_V), (C_V, C_G), (C_G, C_LR), (C_LR, IN_W)):
            for dst, src, end in ((S_KB, C_KB, IN_W), (S_LR, C_LR, C_QB), (S_QB, C_QB, C_KB)) if lo == C_LR else ((lo, lo, hi),):
                sp.dma_start(w_in[:, :, dst:dst + end - src], A["w_in"][0, :, src:end].rearrange("(k p) n -> p k n", p=P))\
                    .then_inc(sem("w_qb_loaded" if src == C_QB else f"w_in_loaded{lo}"), 16)
            if lo == C_V:
                for dst, src in [(b_tm[:, 0:C_LR], A["b_in"][0:1, 0:C_LR].to_broadcast([P, C_LR])),
                                 (b_tm_vb[:, 0:2 * HD], A["b_in"][0:1, C_VB:IN_W].to_broadcast([P, 2 * HD])),
                                 (b_tm_vb[:, 2 * HD:], A["b_in"][0:1, C_LR:C_QB].to_broadcast([P, LOWRANK])),
                                 (b_fm[:, :], A["b_fm"]), (w_a2[:, :], A["w_a2"]),
                                 (sinks[:, :], A["swa_sinks"].to_broadcast([P, HB])),
                                 (gnorm[:, :], A["gla_norm_w"].to_broadcast([P, DV])),
                                 (cums[:, :, :], A["c_cums"]), (cind[:, :], A["c_cind"]),
                                 (causal[:, :], A["c_causal"]),
                                 (alibi[:, :, :], A["c_alibi"])]:
                    sp.dma_start(dst, src).then_inc(sem("consts"), 16)
                sp.wait_ge(sem("xn_ready"), 1)
                sp.dma_start(x[:, :], A["x"][P:2 * P, :]).then_inc(sem("x_loaded"), 16)
        sp.dma_start(w_out[:, :, :], A["w_out"][0].rearrange("(k p) n -> p k n", p=P)).then_inc(sem("w_out_loaded"), 16)
        sp.dma_start(w_r[:, :, 0:NG], A["w_group"][0].rearrange("(k p) n -> p k n", p=P)).then_inc(sem("w_out_loaded"), 16)
        sp.dma_start(w_r[:, :, NG:NR], A["w_router"][0].rearrange("(k p) n -> p k n", p=P)).then_inc(sem("w_out_loaded"), 16)
        sp.dma_start(b_r[:, 0:NG], A["b_group"].to_broadcast([P, NG])).then_inc(sem("w_out_loaded"), 16)
        sp.dma_start(b_r[:, NG:NR], A["b_router"].to_broadcast([P, NE])).then_inc(sem("w_out_loaded"), 16)

    def clear_y(sp, i):
        blocks = scratch["y"].rearrange("(b p) (r c) -> b p r c", p=P, c=128)
        src = nought[:, None, :].to_broadcast([P, D // 128, 128])
        n = NE // NT
        for m in range(n):
            for b in (2 * (n * i + m) + 1, 2 * NE + n * i + m):
                dst = blocks[b] if isinstance(b, int) else blocks[bass.ds(b, 1)].rearrange("o p r c -> (o p) r c")
                sp.dma_start(dst, src).then_inc(sem("y_cleared"), 16)

    FIRST, CONSTS, W_OUT = 5 * 16, 11 * 16, 5 * 16

    rider = (sem("first_consts"), FIRST)

    def tile_rows(ap, t):
        return ap[t * P:(t + 1) * P, :] if isinstance(t, int) else ap[bass.ds(t * P, P), :]

    def sp_iter(sp, i, par):
        if not isinstance(i, int) or 1 <= i < NT - 1:
            wait_apart(sp, rider, (sem("xn_ready"), i + 1))
            nxt = i + 1 if isinstance(i, int) else (i + 1) & (NT - 1)
            sp.dma_start(x[:, :], tile_rows(A["x"], nxt)).then_inc(sem("x_loaded"), 16)
        if not isinstance(i, int) or i < NT:
            clear_y(sp, i)
            wait_apart(sp, rider, (sem("h_stored"), 16 * (i - 1)),
                       (sem("v2_ready"), i - 1))
            sp.dma_start(h[:, par, :], tile_rows(A["x"], i)).then_inc(sem("xr_loaded"), 16)
        if not isinstance(i, int) or 1 <= i <= NT:
            wait_apart(sp, rider, (sem("h_ready"), 2 * i))
            sp.dma_start(tile_rows(scratch["h"], i - 1), h[:, 1 - par, :]).then_inc(sem("h_stored"), 16)
            wait_apart(sp, rider, (sem("v2_ready"), i))
            sp.dma_start(tile_rows(scratch["v2"], i - 1), v2[:, :]).then_inc(sem("v2_stored"), 16)

    def runs(k, i):
        lag = JOBS[k][1]
        return not isinstance(i, int) or 0 <= i - lag < NT + (lag < 0)

    def bank_free(k, i):
        j, it = k, i
        for _ in range(12):
            j -= 8
            if j < 0:
                j, it = j + len(JOBS), it - 1
            if isinstance(it, int) and it < -1:
                return []
            if runs(j, it):
                name, lag, taken = JOBS[j]
                return [(sem(s), (it - lag) * per + nth) for s, (per, nth) in taken.items()]
        return []

    def pe_iter(pe, i, par):
        bk = {name: bank[k % 8] for k, (name, _, _) in enumerate(JOBS)}

        def on(name):
            k = INDEX[name]
            if not runs(k, i):
                return False
            for s, n in bank_free(k, i):
                wait(pe, s, n)
            return True

        def transposes(name, src, n):
            for c in range(n):
                m = pe.transpose(bk[name][:, c * P:(c + 1) * P], src(c), ident)
            m.then_inc(sem(name + "_done"), 1)

        def project(name, lo, hi, col=0, stop_inc=True):
            for k in range(KD):
                m = pe.matmul(bk[name][:, col:col + hi - lo], uT[:, k, :], w_in[:, k, lo:hi],
                              start=k == 0, stop=k == KD - 1)
            return m

        def project_T(name, lo, hi, col):
            for k in range(KD):
                m = pe.matmul(bk[name][0:hi - lo, col:col + P], w_in[:, k, lo:hi], uT[:, k, :],
                              start=k == 0, stop=k == KD - 1)
            return m

        def transpose_x(t):
            wait(pe, sem("xn_ready"), t + 1)
            transposes("xTa", lambda c: xn[:, c * P:(c + 1) * P], 4)
            if not (isinstance(t, int) and t == 0):
                on("xTb")
            transposes("xTb", lambda c: xn[:, (4 + c) * P:(5 + c) * P], 4)

        if isinstance(i, int) and i == 0:
            transpose_x(0)
        if on("qk"):
            if isinstance(i, int) and i == 0:
                wait(pe, sem(f"w_in_loaded{C_QK}"), 16)
            wait(pe, sem("uT_ready"), 2 * i + 2)
            project("qk", C_QK, C_V).then_inc(sem("qk_done"), 1)
        if on("qdki"):
            wait(pe, sem("qdki_ready"), i)
            for c in range(2):
                pe.transpose(bk["qdki"][:, c * P:(c + 1) * P], qd[:, c * P:(c + 1) * P], ident)
            for c in range(2):
                m = pe.transpose(bk["qdki"][:, (2 + c) * P:(3 + c) * P], ki[:, c * P:(c + 1) * P], ident)
            m.then_inc(sem("qdki_done"), 1)
        if on("u2Ta"):
            wait(pe, sem("v2_ready"), i - 1)
            transposes("u2Ta", lambda c: v2[:, c * P:(c + 1) * P], 4)
        if on("u2Tb"):
            transposes("u2Tb", lambda c: v2[:, (4 + c) * P:(5 + c) * P], 4)
        for a in range(2):
            name = f"att{a}"
            if on(name):
                wait(pe, sem("qdkiT_ready"), i)
                r = slice(64 * a, 64 * a + 64)
                for pr in range(2):
                    m = pe.matmul(bk[name][:, pr * P:(pr + 1) * P], qdkiT[r, 2 + pr, :], qdkiT[r, pr, :],
                                  start=True, stop=True)
                m.then_inc(sem("att_done"), 1)
        for c in range(2):
            name = f"dS{c}"
            if runs(INDEX[name], i):
                wait_apart(pe, rider, *bank_free(INDEX[name], i), (sem("ke_ready"), i))
                r = slice(64 * c, 64 * c + 64)
                for hh in range(HA):
                    a, pr = hh % 2, hh // 2
                    m = pe.matmul(bk[name][64 * a:64 * a + 64, pr * DV:(pr + 1) * DV],
                                  ke[r, hh * DK:(hh + 1) * DK], v[r, 1 - par, hh * DV:(hh + 1) * DV],
                                  start=True, stop=True)
                m.then_inc(sem("dS_done"), 1)
        if on("v"):
            if isinstance(i, int) and i == 0:
                wait(pe, sem(f"w_in_loaded{C_V}"), 16)
            project("v", C_V, C_G).then_inc(sem("v_done"), 1)
        if on("router"):
            if isinstance(i, int):
                wait(pe, sem("w_out_loaded"), W_OUT)
            wait(pe, sem("u2T_ready"), 2 * (i - 2) + 2)
            for k in range(KD):
                m = pe.matmul(bk["router"][:, 0:NR], u2T[:, k, :], w_r[:, k, :], start=k == 0, stop=k == KD - 1)
            m.then_inc(sem("router_done"), 1)
        if on("pTp"):
            wait(pe, sem("p_ready"), 2 * i)
            transposes("pTp", lambda c: pp[:, 2 * c:2 * c + 2, :].rearrange("p h j -> p (h j)"), 4)
        for n in range(2):
            if on(f"pTc{n}"):
                transposes(f"pTc{n}", lambda c: sc[:, 4 * n + c, CHUNK:], 4)
        if on("g"):
            if isinstance(i, int) and i == 0:
                wait(pe, sem(f"w_in_loaded{C_G}"), 16)
            project("g", C_G, C_LR).then_inc(sem("g_done"), 1)
        for a in range(2):
            name = f"og{a}"
            if on(name):
                wait(pe, sem("att_ready"), 2 * (i - 1) + a + 1)
                wait(pe, sem("Smid_ready"), i)
                for pr in range(2):
                    hh = 2 * pr + a
                    o = slice(pr * DV, (pr + 1) * DV)
                    r = slice(64 * a, 64 * a + 64)
                    pe.matmul(bk[name][:, o], attm[:, hh, :], v[:, 1 - par, hh * DV:(hh + 1) * DV],
                              start=True, stop=False, skip_group_check=True)
                    pe.matmul(bk[name][0:64, o], qdkiT[r, pr, 0:64], S[r, 1 - par, pr, :],
                              start=False, stop=True, skip_group_check=True)
                    m = pe.matmul(bk[name][64:128, o], qdkiT[r, pr, 64:128], Smid[r, pr, :],
                                  start=False, stop=True, skip_group_check=True)
                m.then_inc(sem("og_done"), 1)
        for a in range(2):
            name = f"ob{a}"
            if on(name):
                wait(pe, sem("pT_ready"), 3 * i)
                wait(pe, sem("vlo_ready"), i - 1)
                r = slice(64 * a, 64 * a + 64)
                first_tile = isinstance(i, int) and i == 1
                for pr in range(4):
                    hh = 2 * pr + a
                    gg = hh // 4
                    m = pe.matmul(bk[name][r, pr * P:(pr + 1) * P], vb[:, 1 - par, gg * HD:(gg + 1) * HD],
                                  pTc[:, hh, :], start=True, stop=first_tile, skip_group_check=True)
                    if not first_tile:
                        vp = vlo[:, gg * HD:(gg + 1) * HD] if a == 0 else vb[64:128, par, gg * HD:(gg + 1) * HD]
                        m = pe.matmul(bk[name][r, pr * P:(pr + 1) * P], vp, pTp[r, pr, :],
                                      start=False, stop=True, skip_group_check=True)
                m.then_inc(sem("ob_done"), 1)
        if on("kv"):
            if isinstance(i, int) and i == 0:
                wait(pe, sem(f"w_in_loaded{C_LR}"), 2 * 16)
            project_T("kv", S_KB, S_VB, 0)
            project("kv", S_VB, IN_W, col=P).then_inc(sem("kv_done"), 1)
        if on("mixAT"):
            wait(pe, sem("mixA_ready"), i)
            transposes("mixAT", lambda c: mixA[:, c * P:(c + 1) * P], 4)
        if on("qb"):
            if isinstance(i, int) and i == 0:
                wait(pe, sem("w_qb_loaded"), 16)
            for m_ in range(4):
                m = project_T("qb", S_QB + m_ * P, S_QB + (m_ + 1) * P, m_ * P)
                if m_ == 0:
                    on("la")
                    wait(pe, sem("vb_ready"), i + 1)
                    pe.transpose(bk["la"][0:LOWRANK, QKA:QKA + P], vb[:, par, 2 * HD:], ident).then_inc(sem("lrT_done"), 1)
                if m_ == 2:
                    wait(pe, sem("lrT_ready"), i + 1)
                    pe.matmul(bk["la"][:, 0:QKA], lrT[:, :], w_a2[:, :], start=True, stop=True).then_inc(sem("la_done"), 1)
            m.then_inc(sem("qb_done"), 1)
        if (not isinstance(i, int) or i + 1 < NT) and on("xTa"):
            transpose_x(i + 1)
        for n in range(2):
            if on(f"wo{n}"):
                if isinstance(i, int) and i == 1 and n == 0:
                    wait(pe, sem("w_out_loaded"), W_OUT)
                wait(pe, sem("ob_taken"), 2 * i)
                wait(pe, sem("mixAT_taken"), i)
                for k in range(KD):
                    m = pe.matmul(bk[f"wo{n}"][:, :], mixT[:, k, :], w_out[:, k, n * 512:(n + 1) * 512],
                                  start=k == 0, stop=k == KD - 1)
                m.then_inc(sem("wo_done"), 1)
        for n in range(4):
            name, gg, r = f"s{n}", n // 2, slice(64 * (n % 2), 64 * (n % 2) + 64)
            if on(name):
                wait(pe, sem("qbT_ready"), i + 1)
                wait(pe, sem("kb_ready"), i + 1)
                for m_ in range(2):
                    m = pe.matmul(bk[name][:, m_ * WK:(m_ + 1) * WK], qbT[r, 2 * gg + m_, :], kb[r, gg, :], start=True, stop=True)
                m.then_inc(sem("s_done"), 1)
        if on("bb"):
            wait(pe, sem("ls_ready"), i + 1)
            for n in range(2):
                m = pe.matmul(bk["bb"][:, n * QKA:(n + 1) * QKA], cums[:, n, :], ls[:, :], start=True, stop=True)
            m.then_inc(sem("bb_done"), 1)
        if on("bl"):
            for pr in range(2):
                m = pe.matmul(bk["bl"][:, 2 * pr:2 * pr + 2], ls[:, pr * P:(pr + 1) * P], cind[:, :],
                              start=True, stop=True)
            m.then_inc(sem("bl_done"), 1)

    BK = {name: bank[k % 8] for k, (name, _, _) in enumerate(JOBS)}

    def act_iter(act, i, par):
        old = not isinstance(i, int) or 1 <= i <= NT
        new = not isinstance(i, int) or i < NT

        def square(t):
            wait(act, sem("x_loaded"), 16 * (t + 1))
            wait(act, sem("ss2_ready"), t - 2)
            act.activation(junk[:, :], x[:, :], ACT.Square, accum_out=ss[:, 0:1]).then_inc(sem("ss1_ready"), 1)

        if isinstance(i, int) and i == 0:
            square(0)
        if old:
            wait(act, sem("qdki_done"), i)
            wait(act, sem("og_done"), 2 * (i - 1))
            act.activation(qdkiT[:, :, :].rearrange("p a b -> p (a b)"), BK["qdki"][:, :], ACT.Copy)\
                .then_inc(sem("qdkiT_ready"), 1)
            for n, (name, dst) in enumerate((("pTp", pTp[:, :, :]), ("pTc0", pTc[:, 0:4, :]), ("pTc1", pTc[:, 4:8, :]))):
                wait(act, sem(name + "_done"), i)
                wait(act, sem("ob_done"), 2 * (i - 1))
                act.activation(dst.rearrange("p a b -> p (a b)"), BK[name][:, :], ACT.Copy).then_inc(sem("pT_ready"), 1)
        if not isinstance(i, int) or i + 1 < NT:
            wait(act, sem("rstd1_ready"), i + 1)
            square(i + 1)
        if old:
            for a in range(2):
                wait(act, sem("og_done"), 2 * (i - 1) + a + 1)
                if a == 0:
                    wait(act, sem("ss1_ready"), min(i + 2, NT) if isinstance(i, int) else i + 2)
                for pr in range(2):
                    hh = 2 * pr + a
                    m = act.activation(junk[:, hh * DV:(hh + 1) * DV], BK[f"og{a}"][:, pr * DV:(pr + 1) * DV], ACT.Square,
                                       accum_out=ss[:, 4 + hh:5 + hh])
                m.then_inc(sem("ssg_ready"), 1)
            for a in range(2):
                wait(act, sem("ob_done"), 2 * (i - 1) + a + 1)
                wait(act, sem("wo_done"), 2 * (i - 1))
                r = slice(64 * a, 64 * a + 64)
                act.activation(mixT[r, 4:8, :].rearrange("p a b -> p (a b)"), BK[f"ob{a}"][r, :], ACT.Copy)\
                    .then_inc(sem("ob_taken"), 1)
        if new:
            wait(act, sem("kv_done"), i + 1)
            if isinstance(i, int) and i == 0:
                wait(act, sem("consts"), CONSTS)
                wait(act, sem("filled"), 5)
            wait(act, sem("qk_ready"), i + 1)
            act.activation(kb[0:64, 0, CHUNK:], BK["kv"][0:64, 0:P], ACT.Identity, bias=b_fm[0:64, 4:5])\
                .then_inc(sem("kb_halves"), 1)
            act.activation(kb[64:128, 1, CHUNK:], BK["kv"][64:128, 0:P], ACT.Identity, bias=b_fm[64:128, 4:5])\
                .then_inc(sem("kb_taken"), 1)
        if old:
            wait(act, sem("mixAT_done"), i)
            act.activation(mixT[:, 0:4, :].rearrange("p a b -> p (a b)"), BK["mixAT"][:, :], ACT.Copy)\
                .then_inc(sem("mixAT_taken"), 1)
        if new:
            wait(act, sem("lrT_done"), i + 1)
            wait(act, sem("la_done"), i)
            act.activation(lrT[0:LOWRANK, :], BK["la"][0:LOWRANK, QKA:QKA + P], ACT.Copy).then_inc(sem("lrT_ready"), 1)
            wait(act, sem("la_done"), i + 1)
            wait(act, sem("ls_ready"), i)
            act.activation(la_t[:, :], BK["la"][:, 0:QKA], ACT.Abs).then_inc(sem("la_abs"), 1)
            act.wait_ge(sem("la_abs"), 2 * i + 1)
            act.activation(la_t[:, :], la_t[:, :], ACT.Exp, scale=-1.0).then_inc(sem("la_abs"), 1)
            act.wait_ge(sem("la_abs"), 2 * i + 2)
            act.activation(la_t[:, :], la_t[:, :], ACT.Ln, bias=1.0).then_inc(sem("la_ln"), 1)
            wait(act, sem("qb_done"), i + 1)
            for n in range(4):
                m = act.activation(qbT[:, n, :], BK["qb"][:, n * P:(n + 1) * P], ACT.Identity, bias=b_fm[:, n:n + 1])
            m.then_inc(sem("qbT_ready"), 1)
            wait(act, sem("g_ready"), i + 1)
            wait(act, sem("gm_ready"), i)
            act.activation(g_t[:, :], g[:, :], ACT.Abs).then_inc(sem("g_abs"), 1)
            act.wait_ge(sem("g_abs"), 2 * i + 1)
            act.activation(g_t[:, :], g_t[:, :], ACT.Exp, scale=-1.0).then_inc(sem("g_abs"), 1)
            act.wait_ge(sem("g_abs"), 2 * i + 2)
            act.activation(g_t[:, :], g_t[:, :], ACT.Ln, bias=1.0).then_inc(sem("g_ln"), 1)
        if old:
            wait(act, sem("h_ready"), 2 * i)
            wait(act, sem("ssg_ready"), 2 * i)
            act.activation(junk[:, :], h[:, 1 - par, :], ACT.Square, accum_out=ss[:, 8:9]).then_inc(sem("ss2_ready"), 1)
        if new:
            wait(act, sem("lsg_ready"), i + 1)
            act.activation(g_t[:, :], g_t[:, :], ACT.Exp).then_inc(sem("sig_ready"), 1)
            wait(act, sem("bb_done"), i + 1)
            wait(act, sem("ke_ready"), i)
            act.activation(E[:, 0:2, :].rearrange("p a b -> p (a b)"), BK["bb"][:, :], ACT.Exp)
            act.activation(E[:, 2, :], BK["bb"][:, 0:QKA], ACT.Exp, scale=-1.0).then_inc(sem("decays_ready"), 1)
            wait(act, sem("bl_done"), i + 1)
            wait(act, sem("S_ready"), i)
            act.activation(dec[:, :], BK["bl"][:, 0:4], ACT.Exp).then_inc(sem("dec_ready"), 1)
            wait(act, sem("nm_ready"), i + 1)
            for hh in range(HB):
                act.activation(sc[:, hh, :], sc[:, hh, :], ACT.Exp, bias=nm[:, hh:hh + 1], accum_out=sums[:, hh:hh + 1])
            act.activation(esink, esink, ACT.Exp).then_inc(sem("exps_ready"), 1)

    def dve_iter(v_, i, par):
        old = not isinstance(i, int) or 1 <= i <= NT
        new = not isinstance(i, int) or i < NT
        old2 = not isinstance(i, int) or 2 <= i
        dve = nc.vector

        def normalise_x(t):
            wait(v_, sem("rstd1_ready"), t + 1)
            if not isinstance(t, int) or t >= 1:
                wait(v_, sem("xTb_done"), t)
            dve.tensor_scalar(xn[:, :], x[:, :], ss[:, 1:2], None, ALU.mult).then_inc(sem("xn_ready"), 1)

        def spread_x(t):
            for n, name in enumerate(("xTa", "xTb")):
                wait(v_, sem(name + "_done"), t + 1)
                wait(v_, sem("qb_done"), t)
                dve.tensor_tensor(uT[:, 4 * n:4 * n + 4, :], BK[name][:, :].rearrange("p (a b) -> p a b", a=4),
                                  norm1[:, 4 * n:4 * n + 4].unsqueeze(2).to_broadcast([P, 4, P]), ALU.mult)\
                    .then_inc(sem("uT_ready"), 1)

        if isinstance(i, int) and i == 0:
            dve.memset(nought[:, :], 0.0).then_inc(sem("filled"), 1)
            dve.memset(lrT[:, :], 1.0).then_inc(sem("filled"), 1)
            dve.memset(attm[:, :, :], 0.0).then_inc(sem("filled"), 1)
            dve.memset(S[:, 0, :, :], 0.0).then_inc(sem("filled"), 1)
            dve.memset(kb[:, :, 0:CHUNK], 0.0).then_inc(sem("filled"), 1)
            wait(v_, sem("first_consts"), FIRST)
            normalise_x(0)
            spread_x(0)
        if old:
            wait(v_, sem("decays_ready"), i)
            wait(v_, sem("qdki_done"), i - 1)
            wait(v_, sem("dS_done"), 2 * (i - 1))
            dve.scalar_tensor_tensor(qd[:, :], qk[:, 0:QKA], DK ** -0.5, E[:, 0, :], ALU.mult, ALU.mult)
            dve.tensor_tensor(ki[:, :], qk[:, QKA:], E[:, 2, :], ALU.mult).then_inc(sem("qdki_ready"), 1)
            dve.tensor_tensor(ke[:, :], qk[:, QKA:], E[:, 1, :], ALU.mult).then_inc(sem("ke_ready"), 1)
            wait(v_, sem("exps_ready"), i)
            dve.tensor_tensor(den, sums, esink, ALU.add).then_inc(sem("den_steps"), 1)
            v_.wait_ge(sem("den_steps"), 2 * (i - 1) + 1)
            dve.reciprocal(rden, den).then_inc(sem("den_steps"), 1)
            v_.wait_ge(sem("den_steps"), 2 * (i - 1) + 2)
            wait(v_, sem("gm_ready"), i)
            for dst, lo, hi in ((pp[:, :, :], 0, CHUNK), (sc[:, :, CHUNK:], CHUNK, WK)):
                dve.tensor_tensor(dst, sc[:, :, lo:hi], rden.unsqueeze(2).to_broadcast([P, HB, hi - lo]), ALU.mult)\
                    .then_inc(sem("p_ready"), 1)
        if new:
            if isinstance(i, int) and i == 0:
                wait(v_, sem("consts"), CONSTS)
            if not isinstance(i, int) or i >= 1:
                wait(v_, sem("s_done"), 4 * i)
                dve.tensor_copy(kb[:, :, 0:CHUNK], kb[:, :, P:WK])
            wait(v_, sem("qk_done"), i + 1)
            dve.tensor_tensor(qk[:, :], BK["qk"][:, :], b_tm[:, C_QK:C_V], ALU.add).then_inc(sem("qk_ready"), 1)
        if old2:
            for n, name in enumerate(("u2Ta", "u2Tb")):
                wait(v_, sem(name + "_done"), i - 1)
                wait(v_, sem("router_done"), i - 2)
                dve.tensor_tensor(u2T[:, 4 * n:4 * n + 4, :], BK[name][:, :].rearrange("p (a b) -> p a b", a=4),
                                  norm2[:, 4 * n:4 * n + 4].unsqueeze(2).to_broadcast([P, 4, P]), ALU.mult)\
                    .then_inc(sem("u2T_ready"), 1)
        if old:
            for a in range(2):
                if isinstance(i, int) and i == 1:
                    wait(v_, sem("filled"), 5)
                wait_apart(v_, rider, (sem("og_done"), 2 * (i - 1)),
                           (sem("att_done"), 2 * (i - 1) + a + 1))
                dve.copy_predicated(attm[:, a::2, :], causal[:, None, :].to_broadcast([P, 2, P]),
                                    BK[f"att{a}"][:, 0:2 * P].rearrange("p (a b) -> p a b", a=2))\
                    .then_inc(sem("att_ready"), 1)
        if old:
            wait(v_, sem("dS_done"), 2 * (i - 1) + 2)
            wait(v_, sem("dec_ready"), i)
            for pr in range(2):
                m = dve.scalar_tensor_tensor(Smid[:, pr, :], S[:, 1 - par, pr, :], dec[:, 2 * pr:2 * pr + 1],
                                             BK["dS0"][:, pr * DV:(pr + 1) * DV], ALU.mult, ALU.add)
            m.then_inc(sem("Smid_ready"), 1)
            v_.wait_ge(sem("Smid_ready"), i)
            for pr in range(2):
                m = dve.scalar_tensor_tensor(S[:, par, pr, :], Smid[:, pr, :], dec[:, 2 * pr + 1:2 * pr + 2],
                                             BK["dS1"][:, pr * DV:(pr + 1) * DV], ALU.mult, ALU.add)
            m.then_inc(sem("S_ready"), 1)
        if new:
            wait(v_, sem("v_done"), i + 1)
            dve.tensor_tensor(v[:, par, :], BK["v"][:, :], b_tm[:, C_V:C_G], ALU.add).then_inc(sem("v_ready"), 1)
            if not isinstance(i, int) or i + 1 < NT:
                normalise_x(i + 1)
        if old2:
            wait(v_, sem("router_done"), i - 1)
            t = i - 2
            dst = logits[:, t, :] if isinstance(t, int) else logits[:, bass.ds(t, 1), :].rearrange("p o n -> p (o n)")
            dve.tensor_tensor(dst, BK["router"][:, 0:NR], b_r[:, :], ALU.add).then_inc(sem("logits_ready"), 1)
        if new:
            wait(v_, sem("g_done"), i + 1)
            wait(v_, sem("gm_ready"), i)
            dve.tensor_tensor(g[:, :], BK["g"][:, :], b_tm[:, C_G:C_LR], ALU.add).then_inc(sem("g_ready"), 1)
        if old:
            wait(v_, sem("rstdg_ready"), i)
            wait(v_, sem("mixAT_done"), i - 1)
            wait(v_, sem("gm_ready"), i)
            for a in range(2):
                dve.tensor_tensor(mixA[:, :].rearrange("p (a c b) -> p a c b", a=2, c=2)[:, :, a, :],
                                  BK[f"og{a}"][:, 0:2 * DV].rearrange("p (a b) -> p a b", a=2),
                                  ss[:, 12 + a:16:2].unsqueeze(2).to_broadcast([P, 2, DV]), ALU.mult)\
                    .then_inc(sem("og_taken"), 1)
            v_.wait_ge(sem("og_taken"), 2 * i)
            dve.tensor_tensor(mixA[:, :], mixA[:, :], gm[:, :], ALU.mult).then_inc(sem("mixA_ready"), 1)
        if new:
            wait(v_, sem("kb_taken"), i + 1)
            wait(v_, sem("ob_done"), 2 * i)
            dve.tensor_tensor(vb[:, par, :], BK["kv"][:, P:2 * P + LOWRANK], b_tm_vb, ALU.add).then_inc(sem("vb_ready"), 1)
            if not isinstance(i, int) or i >= 1:
                dve.tensor_copy(vlo[:, :], vb[64:128, 1 - par, 0:2 * HD]).then_inc(sem("vlo_ready"), 1)
            wait(v_, sem("kb_halves"), i + 1)
            dve.tensor_copy(kb[64:128, 0, CHUNK:], kb[0:64, 0, CHUNK:])
            dve.tensor_copy(kb[0:64, 1, CHUNK:], kb[64:128, 1, CHUNK:]).then_inc(sem("kb_ready"), 1)
            wait(v_, sem("la_ln"), i + 1)
            wait(v_, sem("bl_done"), i)
            dve.scalar_tensor_tensor(ls[:, :], BK["la"][:, 0:QKA], 0.0, la_t[:, :], ALU.min, ALU.subtract)\
                .then_inc(sem("ls_ready"), 1)
            if not isinstance(i, int) or i + 1 < NT:
                spread_x(i + 1)
        if old:
            wait(v_, sem("xr_loaded"), 16 * i)
            for n in range(2):
                wait(v_, sem("wo_done"), 2 * (i - 1) + n + 1)
                hs = h[:, 1 - par, n * 512:(n + 1) * 512]
                dve.tensor_tensor(hs, BK[f"wo{n}"][:, :], hs, ALU.add).then_inc(sem("h_ready"), 1)
        if new:
            wait(v_, sem("g_ln"), i + 1)
            dve.scalar_tensor_tensor(g_t[:, :], g[:, :], 0.0, g_t[:, :], ALU.min, ALU.subtract).then_inc(sem("lsg_ready"), 1)
            wait(v_, sem("pTc1_done"), i)
            for n in range(4):
                wait(v_, sem("s_done"), 4 * i + n + 1)
                heads = slice(4 * (n // 2) + n % 2, 4 * (n // 2) + 4, 2)
                dve.scalar_tensor_tensor(sc[:, heads, :], BK[f"s{n}"][:, 0:2 * WK].rearrange("p (a b) -> p a b", a=2),
                                         HD ** -0.5, alibi[:, heads, :], ALU.mult, ALU.add).then_inc(sem("s_taken"), 1)
            v_.wait_ge(sem("s_taken"), 4 * i + 4)
            if isinstance(i, int) and i == 0:
                dve.memset(sc[:, :, 0:CHUNK], NEG).then_inc(sem("filled"), 1)
                v_.wait_ge(sem("filled"), 6)
            dve.tensor_reduce(m_, sc[:, :, :], AX.X, ALU.max).then_inc(sem("max_steps"), 1)
            v_.wait_ge(sem("max_steps"), 2 * i + 1)
            dve.tensor_tensor(m_, m_, sinks[:, :], ALU.max).then_inc(sem("max_steps"), 1)
            v_.wait_ge(sem("max_steps"), 2 * i + 2)
            dve.tensor_tensor(esink, sinks[:, :], m_, ALU.subtract)
            dve.tensor_scalar(nm, m_, -1.0, None, ALU.mult).then_inc(sem("nm_ready"), 1)
        if old:
            wait(v_, sem("rstd2_ready"), i)
            wait(v_, sem("v2_stored"), 16 * (i - 1))
            wait(v_, sem("u2Tb_done"), i - 1)
            dve.tensor_scalar(v2[:, :], h[:, 1 - par, :], ss[:, 9:10], None, ALU.mult).then_inc(sem("v2_ready"), 1)

    def pool_iter(po, i, par):
        old = not isinstance(i, int) or 1 <= i <= NT
        new = not isinstance(i, int) or i < NT
        pool = nc.gpsimd

        def rstd(ready, done, step, n_ready, n_done, src, dst, width, count, *also):
            wait_apart(po, rider, (sem(ready), n_ready), *also)
            pool.tensor_scalar(src, src, 1.0 / count, EPS, ALU.mult, ALU.add).then_inc(sem(step), 1)
            wait(po, sem(step), n_done)
            pool.tensor_tensor(dst, src, neghalf[:, 0:width], ALU.pow).then_inc(sem(done), 1)

        def rstd_x(t):
            rstd("ss1_ready", "rstd1_ready", "mean1", t + 1, t + 1, ss[:, 0:1], ss[:, 1:2], 1, D,
                 (sem("xn_ready"), t))

        if isinstance(i, int) and i == 0:
            rstd_x(0)
        if not isinstance(i, int) or i + 1 < NT:
            rstd_x(i + 1)
        if old:
            rstd("ssg_ready", "rstdg_ready", "meang", 2 * i, i, ss[:, 4:8], ss[:, 12:16], HA, DV,
                 (sem("mixA_ready"), i - 1))
            rstd("ss2_ready", "rstd2_ready", "mean2", i, i, ss[:, 8:9], ss[:, 9:10], 1, D,
                 (sem("v2_ready"), i - 1))
        if new:
            if isinstance(i, int) and i == 0:
                wait(po, sem("consts"), CONSTS)
            wait(po, sem("mixA_ready"), i)
            wait(po, sem("sig_ready"), i + 1)
            pool.tensor_tensor(gm[:, :], g[:, :], g_t[:, :], ALU.mult).then_inc(sem("gm_step"), 1)
            po.wait_ge(sem("gm_step"), i + 1)
            pool.tensor_tensor(gm[:, :].rearrange("p (a b) -> p a b", a=HA), gm[:, :].rearrange("p (a b) -> p a b", a=HA),
                               gnorm[:, None, :].to_broadcast([P, HA, DV]), ALU.mult).then_inc(sem("gm_ready"), 1)

    return loads, sp_iter, pe_iter, act_iter, dve_iter, pool_iter


def pipeline(eng, step):
    step(eng, 0, 0)
    step(eng, 1, 1)
    with eng.Fori(1, NT // 2) as pair:
        step(eng, 2 * pair, 0)
        step(eng, 2 * pair + 1, 1)
    step(eng, NT, 0)
    step(eng, NT + 1, 1)


def host_constants():
    i, j = np.arange(P)[None, :], np.arange(P)[:, None]
    same = (i // CHUNK) == (j // CHUNK)
    q, k = np.arange(P)[:, None], np.arange(P + CHUNK)[None, :]
    kpos = k - CHUNK
    back = q // CHUNK - np.floor_divide(kpos, CHUNK)
    slopes = 2.0 ** (-8.0 * (np.arange(HB) + 1.0) / HB)
    alibi = np.where((back >= 0) & (back <= 1), -slopes[:, None, None] * np.abs(q - kpos)[None], NEG)
    return {
        "c_ident": np.eye(P, dtype=np.float32),
        "c_cums": np.stack([((j <= i) & same) / 16.0, ((j > i) & same) / 16.0], 1).astype(np.float32),
        "c_cind": (np.arange(P)[:, None] // CHUNK == np.arange(2)[None, :]).astype(np.float32) / 16.0,
        "c_causal": ((j <= i) & same).astype(np.int32),
        "c_alibi": np.ascontiguousarray(alibi.transpose(1, 0, 2)).astype(np.float32),
        "c_neghalf": np.full((P, HA), -0.5, np.float32),
        "c_rank": (j < i).astype(np.float32) - 1.0,
        "c_tie": np.tile(np.arange(EPG, 0, -1, dtype=np.float32), (P, 1)),
        "c_cols": np.tile(np.arange(NE, dtype=np.float32) * CAP, (P, 1)),
        "c_ovj": np.arange(NOV, dtype=np.float32)[None, :],
        "c_tok": (np.arange(NT)[None, :] * P + np.arange(P)[:, None]).astype(np.float32),
        "c_iota": np.tile(np.arange(P, dtype=np.float32), (P, 1)),
    }


def routing(nc, sem, bank, A, K, scratch, ctx):
    def sb(name, shape, dt=F32):
        return ctx.enter_context(nc.sbuf_tensor(name, shape, dt))

    rank_c = sb("rank_c", [P, P])
    ones = sb("ones", [P, P])
    cols = sb("cols", [P, NE])
    ovj = sb("ovj", [1, NOV])
    tok = sb("tok", [P, NT])
    iota = sb("iota", [P, P])
    NCOL = NSLOT // P
    place = sb("place", [P, 2 * NT, P])
    column = sb("column", [P, 2 * NT, NCOL])
    lof, hif = sb("slot_lo_f", [P, 2 * NT]), sb("slot_hi_f", [P, 2 * NT])
    gmax, wsum, gw = sb("gmax", [P, NT]), sb("wsum", [P, NT]), sb("gw", [P, NT])
    eg, ohg, pg = sb("eg", [P, NT, NG]), sb("ohg", [P, NT, NG]), sb("pg", [P, NT, NG])
    big = sb("big", [P, NT, NE])
    el, te = sb("el", [P, NT, EPG]), sb("te", [P, NT, EPG])
    oh = sb("oh", [P, 2, NT, EPG])
    mx = sb("mx", [P, 2, NT])
    OH = sb("OH", [P, 2, NT, NE])
    OHs, OHcum = sb("OHs", [P, NE, NT]), sb("OHcum", [P, NE, NT])
    later = sb("later", [P, NE, NT])
    tot, cnt, nov, cumov, base = (sb(n, [P, NE]) for n in ("tot", "cnt", "nov", "cumov", "base"))
    novi = sb("novi", [P, NE], I32)
    one_row = sb("one_row", [P, NE])
    slot = sb("slot", [P, 2, NT])
    lo, hi = (sb(n, [P, 2, NT], I32) for n in ("slot_lo", "slot_hi"))
    ovc, meta_f = sb("ovc", [1, NOV, NE]), sb("meta_f", [1, NE + NOV + 1])
    logits, gates, dest, idx, meta = K["logits"], K["gates"], K["dest"], K["idx"], K["meta"]
    tie = K["tie"]

    def sp_loads(sp):
        wait(sp, sem("logits_ready"), NT)
        sp.wait_ge(sem("v2_stored"), 16 * NT)
        for dst, src in ((rank_c[:, :], A["c_rank"]), (cols[:, :], A["c_cols"]),
                         (ovj[:, :], A["c_ovj"]), (tok[:, :], A["c_tok"]), (iota[:, :], A["c_iota"])):
            sp.dma_start(dst, src).then_inc(sem("route_consts"), 16)

    def act_part(act):
        act.wait_ge(sem("route_args"), 1)
        act.activation(pg[:, :, :], eg[:, :, :], ACT.Exp).then_inc(sem("route_exps"), 1)
        act.wait_ge(sem("route_args"), 2)
        act.activation(mx[:, 1, :], mx[:, 1, :], ACT.Exp).then_inc(sem("route_exps"), 1)

    def flat(t):
        return t[:, :, :].rearrange("p e t -> p (e t)")

    def pe_part(pe):
        pe.wait_ge(sem("onehots_ready"), 1)
        pe.wait_ge(sem("route_consts"), 5 * 16)
        pe.matmul(bank[0][:, :], rank_c[:, :], flat(OHs), start=True, stop=False)
        pe.matmul(bank[0][:, :], ones[:, :], flat(OHcum), start=False, stop=True)
        pe.matmul(bank[1][:, 0:NE], ones[:, :], tot[:, :], start=True, stop=True).then_inc(sem("ranks_done"), 1)
        for g in range(2 * NT):
            if g % PART == 0:
                pe.wait_ge(sem("columns_ready"), g // PART + 1)
            m = pe.matmul(bank[2][:, 0:NCOL], place[:, g, :], column[:, g, :], start=g == 0, stop=g == 2 * NT - 1)
        m.then_inc(sem("slots_done"), 1)

    PART = 8

    def dve_part(v_):
        dve = nc.vector
        steps = [0]

        def link(ins):
            steps[0] += 1
            ins.then_inc(sem("route_steps"), 1)
            v_.wait_ge(sem("route_steps"), steps[0])

        v_.wait_ge(sem("logits_ready"), NT)
        v_.wait_ge(sem("v2_stored"), 16 * NT)
        v_.wait_ge(sem("h_stored"), 16 * NT)
        dve.memset(ones[:, :], 1.0)
        dve.memset(one_row[:, :], 1.0)
        link(dve.memset(later[:, :, :], 1.0))
        dve.memset(later[:, :, 0], 0.0)
        link(dve.tensor_reduce(gmax[:, :], logits[:, :, 0:NG], AX.X, ALU.max))
        link(dve.tensor_tensor(eg[:, :, :], logits[:, :, 0:NG], gmax[:, :].unsqueeze(2).to_broadcast([P, NT, NG]), ALU.subtract))

        def first_max(out, diff, tmp, m, n):
            link(dve.scalar_tensor_tensor(tmp, diff, 0.0, tie[:, None, EPG - n:EPG].to_broadcast([P, NT, n]), ALU.is_equal, ALU.mult))
            link(dve.tensor_reduce(m, tmp, AX.X, ALU.max))
            link(dve.tensor_tensor(out, tmp, m.unsqueeze(2).to_broadcast([P, NT, n]), ALU.is_equal))

        dve.tensor_copy(wsum[:, :], gmax[:, :]).then_inc(sem("route_args"), 1)
        first_max(ohg[:, :, :], eg[:, :, :], te[:, :, 0:NG], gw[:, :], NG)
        v_.wait_ge(sem("route_exps"), 1)
        link(dve.tensor_reduce(wsum[:, :], pg[:, :, :], AX.X, ALU.add))
        link(dve.reciprocal(gw[:, :], wsum[:, :]))
        ohg_b = ohg[:, :, :].unsqueeze(3).to_broadcast([P, NT, NG, EPG])
        big4 = big[:, :, :].rearrange("p t (g e) -> p t g e", g=NG)
        link(dve.tensor_tensor(big4, logits[:, :, NG:NR].rearrange("p t (g e) -> p t g e", g=NG), ohg_b, ALU.mult))
        link(dve.tensor_reduce(el[:, :, :], big[:, :, :].rearrange("p t (g e) -> p t e g", g=NG), AX.X, ALU.add))
        for n in range(2):
            m = mx[:, n, :]
            link(dve.tensor_reduce(m, el[:, :, :], AX.X, ALU.max))
            link(dve.tensor_tensor(te[:, :, :], el[:, :, :], m.unsqueeze(2).to_broadcast([P, NT, EPG]), ALU.subtract))
            first_max(oh[:, n, :, :], te[:, :, :], te[:, :, :], gmax[:, :], EPG)
            if n == 0:
                link(dve.scalar_tensor_tensor(el[:, :, :], oh[:, 0, :, :], -3.0e38, el[:, :, :], ALU.mult, ALU.add))
        dve.tensor_tensor(mx[:, 1, :], mx[:, 1, :], mx[:, 0, :], ALU.subtract).then_inc(sem("route_args"), 1)
        v_.wait_ge(sem("route_exps"), 2)
        link(dve.tensor_scalar(gmax[:, :], mx[:, 1, :], 1.0, None, ALU.add))
        link(dve.reciprocal(gmax[:, :], gmax[:, :]))
        link(dve.tensor_tensor(gates[:, :, 0], gw[:, :], gmax[:, :], ALU.mult))
        link(dve.tensor_tensor(gates[:, :, 1], gates[:, :, 0], mx[:, 1, :], ALU.mult))
        for n in range(2):
            link(dve.tensor_tensor(OH[:, n, :, :].rearrange("p t (g e) -> p t g e", g=NG), ohg_b,
                                   oh[:, n, :, :].unsqueeze(2).to_broadcast([P, NT, NG, EPG]), ALU.mult))
        link(dve.tensor_tensor(OHs[:, :, :].rearrange("p e t -> p t e"), OH[:, 0, :, :], OH[:, 1, :, :], ALU.add))
        link(dve.tensor_tensor_scan(flat(OHcum), flat(later), flat(OHs), 0.0, ALU.mult, ALU.add))
        dve.tensor_copy(tot[:, :], OHcum[:, :, NT - 1]).then_inc(sem("onehots_ready"), 1)
        v_.wait_ge(sem("ranks_done"), 1)
        v_.wait_ge(sem("route_consts"), 5 * 16)
        link(dve.tensor_copy(cnt[:, :], bank[1][:, 0:NE]))
        link(dve.tensor_scalar(novi[:, :], cnt[:, :], -1.0, 0.0, ALU.add, ALU.max))
        link(dve.tensor_single_scalar(novi[:, :], novi[:, :], 8, ALU.logical_shift_right))
        link(dve.tensor_copy(nov[:, :], novi[:, :]))
        link(dve.tensor_tensor_scan(cumov[:, :], one_row[:, :], nov[:, :], 0.0, ALU.mult, ALU.add))
        link(dve.tensor_tensor(base[:, :], cumov[:, :], nov[:, :], ALU.subtract))
        link(dve.tensor_scalar(base[:, :], base[:, :], float(CAP), float(NE * CAP - CAP), ALU.mult, ALU.add))
        ranks = bank[0][:, :].rearrange("p (e t) -> p t e", e=NE)
        link(dve.tensor_tensor(base[:, :], base[:, :], cols[:, :], ALU.subtract))
        link(dve.tensor_scalar(big[:, :, :], ranks, float(CAP), None, ALU.is_ge))
        link(dve.tensor_tensor(big[:, :, :], big[:, :, :], base[:, None, :].to_broadcast([P, NT, NE]), ALU.mult))
        link(dve.tensor_tensor(big[:, :, :], big[:, :, :], cols[:, None, :].to_broadcast([P, NT, NE]), ALU.add))
        link(dve.tensor_tensor(big[:, :, :], big[:, :, :], ranks, ALU.add))
        for n in range(2):
            dve.tensor_tensor(OH[:, n, :, :], OH[:, n, :, :], big[:, :, :], ALU.mult).then_inc(sem("route_steps"), 1)
            steps[0] += 1
        v_.wait_ge(sem("route_steps"), steps[0])
        f = lambda t: t[:, :, :].rearrange("p a b -> p (a b)")
        link(dve.tensor_reduce(slot[:, :, :], OH[:, :, :, :], AX.X, ALU.add))
        link(dve.tensor_copy(dest, f(slot)))
        link(dve.tensor_single_scalar(f(lo), dest, P - 1, ALU.bitwise_and))
        link(dve.tensor_single_scalar(f(hi), dest, 7, ALU.logical_shift_right))
        dve.tensor_copy(hif[:, :], f(hi))
        link(dve.tensor_copy(lof[:, :], f(lo)))
        for g in range(0, 2 * NT, PART):
            for onehot, n, number in ((place, P, lof), (column, NCOL, hif)):
                m = dve.tensor_tensor(onehot[:, g:g + PART, :], iota[:, None, 0:n].to_broadcast([P, PART, n]),
                                      number[:, g:g + PART].unsqueeze(2).to_broadcast([P, PART, n]), ALU.is_equal)
            m.then_inc(sem("onehots_made"), 1)
        row = meta_f[0:1, 0:NE]
        link(dve.tensor_scalar(row, cnt[0:1, :], float(WIDTHS[0]), None, ALU.is_gt))
        for w in WIDTHS[1:-1]:
            link(dve.scalar_tensor_tensor(row, cnt[0:1, :], float(w), row, ALU.is_gt, ALU.add))
        link(dve.tensor_tensor(ovc[:, :, :], cumov[0:1, None, :].to_broadcast([1, NOV, NE]),
                               ovj[:, :].unsqueeze(2).to_broadcast([1, NOV, NE]), ALU.is_le))
        link(dve.tensor_reduce(meta_f[0:1, NE:NE + NOV], ovc[:, :, :], AX.X, ALU.add))
        link(dve.tensor_scalar(meta_f[0:1, NE:NE + NOV], meta_f[0:1, NE:NE + NOV], float(NE - 1), None, ALU.min))
        link(dve.tensor_copy(meta_f[0:1, NE + NOV:NE + NOV + 1], cumov[0:1, NE - 1:NE]))
        dve.tensor_copy(meta[0:1, 0:NE + NOV + 1], meta_f[0:1, :]).then_inc(sem("meta_ready"), 1)
        v_.wait_ge(sem("slots_done"), 1)
        dve.tensor_copy(idx, bank[2][:, 0:NCOL]).then_inc(sem("idx_ready"), 1)

    def pool_part(po):
        for n, g in enumerate(range(0, 2 * NT, PART)):
            po.wait_ge(sem("onehots_made"), n + 1)
            t = g % NT
            nc.gpsimd.tensor_tensor(column[:, g:g + PART, :], column[:, g:g + PART, :],
                                    tok[:, t:t + PART].unsqueeze(2).to_broadcast([P, PART, NCOL]), ALU.mult)\
                .then_inc(sem("columns_ready"), 1)
        po.wait_ge(sem("idx_ready"), 1)

    return sp_loads, pe_part, act_part, dve_part, pool_part


def experts(nc, sem, bank, A, K, scratch, W, ctx):
    def sb(name, shape, dt=F32):
        return ctx.enter_context(nc.sbuf_tensor(name, shape, dt))

    xT = sb("xT", [P, 2, KD, CAP])
    sg = sb("sg", [P, KF, CAP])
    hT = sb("hT", [P, KF, CAP])
    yT = sb("yT", [P, KD, CAP])
    y = sb("y", [P, 2, 2, D])
    idxc = sb("idxc", [P, 2, 2], I32)
    xg = sb("xg", [P, 2, 2, D])
    ident, norm2, meta, idx = K["ident"], K["norm2"], K["meta"], K["idx"]
    wg, wu, wd = W
    meta_rider = (sem("meta_ready"), 1)
    G, U, XB, YB = bank[0:2], bank[2:4], bank[4:6], bank[6:8]

    def after(eng, pre, name, n):
        eng.wait_ge(sem(pre + name), n + CREDIT)

    def credit(eng, *names):
        for pre in ("m_", "o_"):
            for name in names:
                eng.sem_inc(sem(pre + name), CREDIT)

    def load(sp, pre, which, q, e):
        dst, name = {"g": (wg, "w_gate"), "u": (wu, "w_up"), "d": (wd, "w_down")}[which]
        src = A[name][0, e:e + 1] if isinstance(e, int) else A[name][0, bass.ds(e, 1)]
        sp.dma_start(dst[:, q, :, :], src.rearrange("e (k p) n -> p (e k) n", p=P)).then_inc(sem(f"{pre}{name}_loaded{q}"), 16)

    def store(sp, pre, q, rest, row):
        def rows(lo, n):
            return scratch["y"][row + lo:row + lo + n, :] if isinstance(row, int) else scratch["y"][bass.ds(row + lo, n), :]
        sp.dma_start(rows(0, P), y[:, q, 0, :]).then_inc(sem(f"{pre}y_stored{q}"), 16)
        if rest:
            sp.dma_start(rows(P, rest), y[0:rest, q, 1, :]).then_inc(sem(f"{pre}y_stored{q}"), 16)
        else:
            sp.sem_inc(sem(f"{pre}y_stored{q}"), 16)

    def clear_xg(po):
        po.wait_ge(sem("logits_ready"), NT)
        po.wait_ge(sem("v2_stored"), 16 * NT)
        nc.gpsimd.memset(xg[:, :, 1, :], 0.0).then_inc(sem("xg_cleared"), 1)

    def gather(po, pre, n, q, rest, col):
        for part, rows in ((0, P), (1, rest)):
            po.indirect_dma_start(out=xg[0:rows, q, part, :], in_=scratch["v2"], out_offset=None,
                                  in_offset=bass.IndirectOffsetOnAxis(ap=idxc[0:rows, q, part:part + 1], axis=0))\
                .then_inc(sem(f"{pre}xg_loaded{q}"), 16)

    def copy_index(po, pre, n, q, col):
        wait_apart(po, meta_rider, (sem(pre + "x_done"), 4 * (n - 1) + CREDIT))
        nc.gpsimd.tensor_copy(idxc[:, q, :], idx[:, bass.ds(col, 2)] if not isinstance(col, int) else idx[:, col:col + 2])\
            .then_inc(sem(pre + "index_ready"), 1)
        wait_apart(po, meta_rider, (sem(pre + "index_ready"), n + 1))

    def pe_x(pe, pre, n, q, steps):
        for j in steps:
            if j == 0:
                wait(pe, sem(f"{pre}xg_loaded{q}"), 32 * K["lap"](pre, n, q))
            after(pe, pre, "xT_ready", 4 * n + j - 1)
            for kk in range(2):
                c = slice((2 * j + kk) * P, (2 * j + kk + 1) * P)
                for part in range(2):
                    m = pe.transpose(XB[j % 2][:, kk * CAP + part * P:kk * CAP + (part + 1) * P], xg[:, q, part, c], ident)
            m.then_inc(sem(pre + "x_done"), 1)

    def pe_gu(pe, pre, n, q, w):
        for m_ in range(KF):
            if m_ == 0:
                after(pe, pre, "xT_ready", 4 * n + 4)
                wait(pe, sem(f"{pre}w_gate_loaded{q}"), 16 * K["lap"](pre, n, q))
                wait(pe, sem(f"{pre}w_up_loaded{q}"), 16 * K["lap"](pre, n, q))
            after(pe, pre, "sg_ready", 4 * n + m_ - 1)
            if m_ < 2:
                after(pe, pre, ("yA_taken", "yD_taken")[m_], 2 * n)
                after(pe, pre, "yT_ready", 4 * n)
            for k in range(KD):
                m = pe.matmul(G[m_ % 2][:, 0:w], wg[:, q, k, m_ * P:(m_ + 1) * P], xT[:, q, k, 0:w], start=k == 0, stop=k == KD - 1)
            m.then_inc(sem(pre + "g_done"), 1)
            after(pe, pre, "h_ready", 4 * n + m_ - 1)
            for k in range(KD):
                m = pe.matmul(U[m_ % 2][:, 0:w], wu[:, q, k, m_ * P:(m_ + 1) * P], xT[:, q, k, 0:w], start=k == 0, stop=k == KD - 1)
            m.then_inc(sem(pre + "g_done"), 1)

    def pe_down(pe, pre, n, q, w):
        for j in range(4):
            if j == 0:
                after(pe, pre, "h_ready", 4 * n + 4)
                wait(pe, sem(f"{pre}w_down_loaded{q}"), 16 * K["lap"](pre, n, q))
            after(pe, pre, "yT_ready", 4 * n + j - 1)
            for mm in range(2):
                c = slice((2 * j + mm) * P, (2 * j + mm + 1) * P)
                for k in range(KF):
                    m = pe.matmul(U[j % 2][:, mm * CAP:mm * CAP + w], wd[:, q, k, c], hT[:, k, 0:w],
                                  start=k == 0, stop=k == KF - 1)
            m.then_inc(sem(pre + "d_done"), 1)

    def pe_y(pe, pre, n, w):
        for part in range(2 if w > P else 1):
            for half in range(2):
                after(pe, pre, "yT_ready", 4 * n + 2 * half + 2)
                if part == 0:
                    after(pe, pre, ("yA_taken", "yD_taken")[half], 2 * n)
                for mm in range(4):
                    m = pe.transpose((YB, G)[part][half][:, mm * P:(mm + 1) * P], yT[:, 4 * half + mm, part * P:(part + 1) * P], ident)
                m.then_inc(sem(pre + "yb_done"), 3 if w <= P and half == 1 else 1)

    def pe_chunk(pe, pre, n, q, w, next_x):
        pe_gu(pe, pre, n, q, w)
        next_x((0, 1))
        pe_down(pe, pre, n, q, w)
        next_x((2, 3))
        pe_y(pe, pre, n, w)

    def act_chunk(act, pre, n, q):
        for m_ in range(KF):
            after(act, pre, "g_done", 8 * n + 2 * m_ + 1)
            after(act, pre, "h_ready", 4 * (n - 1) + m_ + 1)
            act.activation(sg[:, m_, :], G[m_ % 2][:, 0:CAP], ACT.Silu).then_inc(sem(pre + "sg_ready"), 1)
        for j in range(4):
            after(act, pre, "d_done", 4 * n + j + 1)
            after(act, pre, "yb_done", 4 * n)
            act.activation(yT[:, 2 * j:2 * j + 2, :], U[j % 2][:, :].rearrange("p (a b) -> p a b", a=2),
                           ACT.Copy).then_inc(sem(pre + "yT_ready"), 1)
        wait(act, sem(f"{pre}y_stored{q}"), 32 * K["lap"](pre, n, q))
        for part in range(2):
            after(act, pre, "yb_done", 4 * n + 2 * part + 1)
            act.activation(y[:, q, part, 0:512], (YB, G)[part][0][:, :], ACT.Copy).then_inc(sem(pre + "yA_taken"), 1)

    def dve_x(v_, pre, n, q):
        for j in range(4):
            after(v_, pre, "x_done", 4 * n + j + 1)
            after(v_, pre, "g_done", 8 * (n - 1))
            nc.vector.tensor_tensor(xT[:, q, 2 * j:2 * j + 2, :], XB[j % 2][:, :].rearrange("p (a b) -> p a b", a=2),
                                    norm2[:, 2 * j:2 * j + 2].unsqueeze(2).to_broadcast([P, 2, CAP]), ALU.mult)\
                .then_inc(sem(pre + "xT_ready"), 1)

    def dve_h(v_, pre, n, q):
        for m_ in range(KF):
            after(v_, pre, "sg_ready", 4 * n + m_ + 1)
            after(v_, pre, "g_done", 8 * n + 2 * m_ + 2)
            after(v_, pre, "d_done", 4 * n)
            nc.vector.tensor_tensor(hT[:, m_, :], U[m_ % 2][:, 0:CAP], sg[:, m_, :], ALU.mult)\
                .then_inc(sem(pre + "h_ready"), 1)

    def dve_y(v_, pre, n, q):
        wait(v_, sem(f"{pre}y_stored{q}"), 32 * K["lap"](pre, n, q))
        for part in range(2):
            after(v_, pre, "yb_done", 4 * n + 2 * part + 2)
            nc.vector.tensor_copy(y[:, q, part, 512:D], (YB, G)[part][1][:, :]).then_inc(sem(pre + "yD_taken"), 1)

    return credit, load, store, clear_xg, gather, copy_index, pe_x, pe_chunk, act_chunk, dve_x, dve_h, dve_y


def by_width(eng, cls, body, of=lambda w: w):
    def among(lo, hi):
        kinds = {of(w) for w in WIDTHS[lo:hi]}
        if len(kinds) == 1:
            body(kinds.pop())
            return
        mid = 1 if lo == 0 else (lo + hi) // 2
        with eng.If(cls < mid):
            among(lo, mid)
        with eng.Else():
            among(mid, hi)
    among(0, len(WIDTHS))


def rest_stored(w):
    return max(w - P, 0)


def rest_gathered(w):
    return max(w - P, 16)


NYG = 4


def combine(nc, sem, A, K, scratch, W, ctx):
    def sb(name, shape, dt=F32):
        return ctx.enter_context(nc.sbuf_tensor(name, shape, dt))

    wgu, wd = W[0], W[1]
    hc = wgu[:, :, :, :, :].rearrange("p w q k n -> p (w q k n)").rearrange("p (t d) -> p t d", d=D)
    yg = wd[:, :, :, :].rearrange("p q k n -> p (q k) n").rearrange("p (b n) d -> p b n d", b=NYG)
    oc = sb("oc", [P, 2, D])
    fw = sb("fw", [P, D])
    fjunk = sb("fjunk", [P, 2, D], BF16)
    dc = sb("dc", [P, NYG, 2], I32)
    gc = sb("gc", [P, NYG, 2])
    fs = sb("fs", [P, NYG, 2])
    nh = sb("nh", [P, HA])
    gates, dest = K["gates"], K["dest"]
    rider = (sem("meta_ready"), 1)
    TPQ = NT // 4

    def tile(ap, t):
        return ap[:, t, :] if isinstance(t, int) else ap[:, bass.ds(t, 1), :].rearrange("p o n -> p (o n)")

    def sp_first(sp):
        sp.dma_start(fw[:, :], A["final_norm_w"].rearrange("(o n) -> o n", o=1).to_broadcast([P, D])).then_inc(sem("fw_loaded"), 16)
        sp.dma_start(nh[:, :], A["c_neghalf"]).then_inc(sem("fw_loaded"), 16)

    def sp_h(sp, q):
        for n in range(2):
            t0 = (2 * n + q) * TPQ
            sp.dma_start(hc[:, t0:t0 + TPQ, :], scratch["h"][t0 * P:(t0 + TPQ) * P, :].rearrange("(t p) d -> p t d", p=P))\
                .then_inc(sem("h_back"), 16)

    def sp_tile(sp, group, n):
        t, q = NYG * group + n, n % 2
        wait_apart(sp, rider, (sem("sum_o_ready"), t + 1))
        dst = A["out"][t * P:(t + 1) * P, :] if isinstance(t, int) else A["out"][bass.ds(t * P, P), :]
        sp.dma_start(dst, oc[:, q, :]).then_inc(sem(f"out_stored{q}"), 16)

    def pool_gather(po, t, b):
        wait_apart(po, rider, (sem("sum_s_ready"), t - NYG + 1 + NYG))
        d = dest.rearrange("p (n t) -> p n t", n=2)
        nc.gpsimd.tensor_copy(dc[:, b, :], d[:, :, t] if isinstance(t, int) else d[:, :, bass.ds(t, 1)].rearrange("p n o -> p (n o)"))\
            .then_inc(sem("sum_dc_ready"), 1)
        wait_apart(po, rider, (sem("sum_dc_ready"), t + 1))
        for n in range(2):
            po.indirect_dma_start(out=yg[:, b, n, :], in_=scratch["y"], out_offset=None,
                                  in_offset=bass.IndirectOffsetOnAxis(ap=dc[:, b, n:n + 1], axis=0)).then_inc(sem(f"yg_loaded{b}"), 16)

    def pool_tile(po, group, n):
        t = NYG * group + n
        if not isinstance(t, int) or t + 2 < NT:
            pool_gather(po, t + 2, (n + 2) % NYG)
        wait_apart(po, rider, (sem("fss_ready"), t + 1))
        nc.gpsimd.tensor_scalar(fs[:, n, 0:1], fs[:, n, 0:1], 1.0 / D, EPS, ALU.mult, ALU.add).then_inc(sem("fmean"), 1)
        wait_apart(po, rider, (sem("fmean"), t + 1))
        nc.gpsimd.tensor_tensor(fs[:, n, 1:2], fs[:, n, 0:1], nh[:, 0:1], ALU.pow).then_inc(sem("froot_ready"), 1)

    def act_tile(act, group, n):
        t = NYG * group + n
        wait(act, sem("sum_s_ready"), t + 1 + NYG)
        act.activation(fjunk[:, n % 2, :], tile(hc, t), ACT.Square, accum_out=fs[:, n, 0:1]).then_inc(sem("fss_ready"), 1)

    def dve_sum(v_, group, n):
        t = NYG * group + n
        nc.vector.tensor_copy(gc[:, n, :], tile(gates, t)).then_inc(sem("sum_steps"), 1)
        v_.wait_ge(sem("sum_steps"), 2 * t + 1)
        v_.wait_ge(sem(f"yg_loaded{n}"), 32 * (group + 1))
        ht = tile(hc, t)
        nc.vector.scalar_tensor_tensor(ht, yg[:, n, 0, :], gc[:, n, 0:1], ht, ALU.mult, ALU.add).then_inc(sem("sum_steps"), 1)
        v_.wait_ge(sem("sum_steps"), 2 * t + 2)
        nc.vector.scalar_tensor_tensor(ht, yg[:, n, 1, :], gc[:, n, 1:2], ht, ALU.mult, ALU.add).then_inc(sem("sum_s_ready"), 1)

    def dve_tile(v_, group, n):
        t, q = NYG * group + n, n % 2
        if not isinstance(t, int) or t + 1 < NT:
            dve_sum(v_, group + (n + 1) // NYG, (n + 1) % NYG)
        v_.wait_ge(sem("froot_ready"), t + 1)
        v_.wait_ge(sem(f"out_stored{q}"), 16 * (2 * group + n // 2) + 16)
        nc.vector.scalar_tensor_tensor(oc[:, q, :], tile(hc, t), fs[:, n, 1:2], fw[:, :], ALU.mult, ALU.mult).then_inc(sem("sum_o_ready"), 1)

    return sp_first, sp_h, sp_tile, pool_gather, pool_tile, act_tile, dve_sum, dve_tile


def tile_groups(eng, step):
    with eng.Fori(0, NT // NYG - 1) as group:
        for n in range(NYG):
            step(eng, group, n)
    for n in range(NYG):
        step(eng, NT // NYG - 1, n)


def program(nc, A):
    with ExitStack() as ctx:
        sem = Semaphores(nc, ctx)
        bank = [ctx.enter_context(nc.psum_tensor(f"bank{n}", [P, 512], F32)) for n in range(8)]

        def sb(name, shape, dt=F32):
            return ctx.enter_context(nc.sbuf_tensor(name, shape, dt))

        ident, norm2, logits = sb("ident", [P, P]), sb("norm2_sb", [P, KD]), sb("logits", [P, NT, NR])
        gates, dest = sb("gates", [P, NT, 2]), sb("dest", [P, 2 * NT], I32)
        tie = sb("tie", [P, EPG])
        idx, meta = sb("idx", [P, NSLOT // P], I32), sb("meta", [1, 64], I32)
        K = {"ident": ident[:, :], "norm2": norm2[:, :], "logits": logits, "tie": tie, "gates": gates, "dest": dest[:, :],
             "idx": idx[:, :], "meta": meta,
             "lap": lambda pre, n, q: (n + 1) if pre == "o_" else ((n - q) // 2 + 1 if isinstance(n, int) else K["pair"] + 1)}
        scratch = {"h": nc.dram_tensor("h_dram", (SEQ, D), F32).ap(), "v2": nc.dram_tensor("v2_dram", (SEQ, D), F32).ap(),
                   "y": nc.dram_tensor("y_dram", (NSLOT, D), F32).ap()}
        with ExitStack() as mem:
            mix_sp_loads, mix_sp, mix_pe, mix_act, mix_dve, mix_pool = mixer(nc, sem, bank, A, K, scratch, mem)
        wgu = ctx.enter_context(nc.sbuf_tensor("wgu", [P, 2, 2, KD, FF], F32))
        wd = ctx.enter_context(nc.sbuf_tensor("wd", [P, 2, KF, D], F32))
        cb_sp_first, cb_sp_h, cb_sp, cb_gather, cb_pool, cb_act, cb_sum, cb_dve = combine(nc, sem, A, K, scratch, (wgu, wd), ctx)
        with ExitStack() as mem:
            rt_sp_loads, rt_pe, rt_act, rt_dve, rt_pool = routing(nc, sem, bank, A, K, scratch, mem)
        with ExitStack() as mem:
            (credit, load, store, clear_xg, gather, copy_index, pe_x, pe_chunk, act_chunk, dve_x, dve_h, dve_y) = \
                experts(nc, sem, bank, A, K, scratch, (wgu[:, 0], wgu[:, 1], wd), mem)
        block = ctx.enter_context(nc.Block())

        def chunk_class(eng, e):
            return eng.value_load(meta[0:1, e:e + 1] if isinstance(e, int) else meta[0:1, bass.ds(e, 1)],
                                  min_val=0, max_val=len(WIDTHS) - 1)

        def lap_is(pair):
            K["pair"] = pair

        def overflow(eng, body, last=None):
            n_over = eng.value_load(meta[0:1, NE + NOV:NE + NOV + 1], min_val=0, max_val=NOV)
            with eng.If(n_over > 0):
                for q in range(2):
                    eng.wait_ge(sem(f"m_y_stored{q}"), 16 * NE + 32)
                eng.nop()
                with eng.Fori(0, NOV) as j:
                    with eng.If(j < n_over):
                        body(j)
                if last:
                    last()
                eng.nop()

        @block.sync
        def _(sp):
            sp.wait_ge(sem("filled"), 1)
            mix_sp_loads(sp)
            for q in range(2):
                sp.sem_inc(sem(f"m_y_stored{q}"), 32)
                sp.sem_inc(sem(f"out_stored{q}"), 16)
            sp.sem_inc(sem("o_y_stored0"), 32)
            mix_sp(sp, 0, 0)
            mix_sp(sp, 1, 1)
            with sp.Fori(1, NT // 2) as pair:
                mix_sp(sp, 2 * pair, 0)
                mix_sp(sp, 2 * pair + 1, 1)
            sp.wait_ge(sem("qb_done"), NT)
            load(sp, "m_", "g", 0, 0)
            mix_sp(sp, NT, 0)
            mix_sp(sp, NT + 1, 1)
            rt_sp_loads(sp)
            cb_sp_first(sp)
            sp.wait_ge(sem("wo_done"), 2 * NT)
            load(sp, "m_", "u", 0, 0)
            load(sp, "m_", "d", 0, 0)
            for which in "gud":
                load(sp, "m_", which, 1, 1)
            sp.wait_ge(sem("meta_ready"), 1)
            sp.wait_ge(sem("y_cleared"), 16 * NE * 2)

            def expert(pair, q):
                lap_is(pair)
                e = 2 * pair + q
                cls = chunk_class(sp, e)
                more = not isinstance(e, int)
                wait_apart(sp, (sem("meta_ready"), 1), (sem("m_g_done"), 8 * e + 8 + CREDIT))
                if more:
                    load(sp, "m_", "g", q, e + 2)
                    load(sp, "m_", "u", q, e + 2)
                    wait_apart(sp, (sem("meta_ready"), 1), (sem("m_d_done"), 4 * e + 4 + CREDIT))
                    load(sp, "m_", "d", q, e + 2)
                else:
                    cb_sp_h(sp, q)
                wait_apart(sp, (sem("meta_ready"), 1), (sem("m_yA_taken"), 2 * e + 2 + CREDIT), (sem("m_yD_taken"), 2 * e + 2 + CREDIT))
                by_width(sp, cls, lambda rest: store(sp, "m_", q, rest, e * CAP), rest_stored)

            with sp.Fori(0, NE // 2 - 1) as pair:
                for q in range(2):
                    expert(pair, q)
            for q in range(2):
                expert(NE // 2 - 1, q)

            def over(j):
                e = sp.value_load(meta[0:1, bass.ds(NE + j, 1)], min_val=0, max_val=NE - 1)
                wait_apart(sp, (sem("h_back"), 4 * 16), (sem("o_d_done"), 4 * j + CREDIT))
                for which in "gud":
                    load(sp, "o_", which, 0, e)
                wait_apart(sp, (sem("meta_ready"), 1), (sem("o_yA_taken"), 2 * j + 2 + CREDIT), (sem("o_yD_taken"), 2 * j + 2 + CREDIT))
                store(sp, "o_", 0, CAP - P, (NE + j) * CAP)

            def h_again():
                cb_sp_h(sp, 0)
                sp.wait_ge(sem("h_back"), 6 * 16)
            overflow(sp, over, h_again)
            sp.wait_ge(sem("h_back"), 4 * 16)
            for q in range(2):
                sp.wait_ge(sem(f"m_y_stored{q}"), 16 * NE + 32)
            sp.sem_inc(sem("h_there"), 1)
            tile_groups(sp, cb_sp)
            for q in range(2):
                sp.wait_ge(sem(f"out_stored{q}"), 16 * (NT // 2 + 1))

        @block.tensor
        def _(pe):
            credit(pe, "x_done", "g_done", "d_done", "yb_done")
            pe.wait_ge(sem("first_consts"), 5 * 16)
            pipeline(pe, mix_pe)
            rt_pe(pe)
            pe.wait_ge(sem("meta_ready"), 1)
            pe_x(pe, "m_", 0, 0, range(4))
            with pe.Fori(0, NE // 2) as pair:
                for q in range(2):
                    e = 2 * pair + q

                    def next_x(steps):
                        lap_is(pair + q)
                        pe_x(pe, "m_", e + 1, 1 - q, steps)
                        lap_is(pair)

                    lap_is(pair)
                    by_width(pe, chunk_class(pe, e), lambda w: pe_chunk(pe, "m_", e, q, w, next_x))

            def over(j):
                pe_x(pe, "o_", j, 0, range(4))
                pe_chunk(pe, "o_", j, 0, CAP, lambda steps: None)
            overflow(pe, over)

        @block.scalar
        def _(act):
            credit(act, "sg_ready", "yT_ready", "yA_taken")
            pipeline(act, mix_act)
            rt_act(act)
            act.wait_ge(sem("meta_ready"), 1)
            with act.Fori(0, NE // 2) as pair:
                lap_is(pair)
                for q in range(2):
                    act_chunk(act, "m_", 2 * pair + q, q)
            overflow(act, lambda j: act_chunk(act, "o_", j, 0))
            tile_groups(act, cb_act)

        @block.vector
        def _(v_):
            credit(v_, "xT_ready", "h_ready", "yD_taken")
            v_.sem_inc(sem("sum_s_ready"), NYG)
            pipeline(v_, mix_dve)
            rt_dve(v_)
            v_.wait_ge(sem("meta_ready"), 1)
            dve_x(v_, "m_", 0, 0)
            with v_.Fori(0, NE // 2) as pair:
                for q in range(2):
                    e = 2 * pair + q
                    lap_is(pair)
                    dve_h(v_, "m_", e, q)
                    dve_x(v_, "m_", e + 1, 1 - q)
                    dve_y(v_, "m_", e, q)

            def over(j):
                dve_x(v_, "o_", j, 0)
                dve_h(v_, "o_", j, 0)
                dve_y(v_, "o_", j, 0)
            overflow(v_, over)
            v_.wait_ge(sem("fw_loaded"), 32)
            v_.wait_ge(sem("h_there"), 1)
            cb_sum(v_, 0, 0)
            tile_groups(v_, cb_dve)

        @block.gpsimd
        def _(po):
            pipeline(po, mix_pool)
            clear_xg(po)
            rt_pool(po)
            po.wait_ge(sem("meta_ready"), 1)
            po.wait_ge(sem("xg_cleared"), 1)
            with po.Fori(0, NE // 2) as pair:
                lap_is(pair)
                for q in range(2):
                    e = 2 * pair + q
                    cls = chunk_class(po, e)
                    copy_index(po, "m_", e, q, 2 * e)
                    by_width(po, cls, lambda rest: gather(po, "m_", e, q, rest, 2 * e), rest_gathered)
            copy_index(po, "m_", NE, 0, 0)
            gather(po, "m_", NE, 0, rest_gathered(0), 0)

            def over(j):
                copy_index(po, "o_", j, 0, 2 * (NE + j))
                gather(po, "o_", j, 0, CAP - P, 0)
                wait_apart(po, (sem("meta_ready"), 1), (sem("o_y_stored0"), 32 * j + 64))
                po.nop()
            overflow(po, over)
            for q in range(2):
                po.wait_ge(sem(f"m_y_stored{q}"), 16 * NE + 32)
            po.wait_ge(sem("m_x_done"), 4 * NE + 4 + CREDIT)
            po.wait_ge(sem("m_xT_ready"), 4 * NE + 4 + CREDIT)
            po.wait_ge(sem("fw_loaded"), 32)
            po.wait_ge(sem("h_there"), 1)
            cb_gather(po, 0, 0)
            cb_gather(po, 1, 1)
            tile_groups(po, cb_pool)


def kernel(**inputs):
    import concourse.bacc as bacc
    from concourse.bass_utils import run_bass_kernel_spmd

    a = {k: np.ascontiguousarray(v) for k, v in inputs.items()}
    a["x"] = a["x"].reshape(SEQ, D)
    a["norm1_t"] = np.ascontiguousarray(a.pop("norm1_w").reshape(KD, P).T)
    a["norm2_t"] = np.ascontiguousarray(a.pop("norm2_w").reshape(KD, P).T)
    b = a["b_in"][0]
    a["b_fm"] = np.ascontiguousarray(np.stack([b[C_QB + n * P:C_QB + (n + 1) * P] for n in range(5)], 1))
    a["w_a2"] = np.concatenate([a.pop("gla_w_a2")[0], a.pop("gla_b_a2")], 0)
    a.update(host_constants())
    nc = bacc.Bacc("TRN2", target_bir_lowering=False, num_devices=1)
    A = {k: nc.dram_tensor(k + "_in", v.shape, mybir.dt.from_np(v.dtype), kind="ExternalInput").ap() for k, v in a.items()}
    A["out"] = nc.dram_tensor("out", (SEQ, D), F32, kind="ExternalOutput").ap()
    program(nc, A)
    r = run_bass_kernel_spmd(nc, [{k + "_in": v for k, v in a.items()}], core_ids=[0])
    return r.results[0]["out"].reshape(1, SEQ, D)
```
